# Optimizing a Trainium2 kernel written in Bass

```python
import jax, jax.numpy as jnp
from jax import lax
import numpy as np

D_MODEL = 4096
BATCH = 1
SEQ = 256
DEPTH = 1

N_MIXERS = 2
N_ATTN_LAYERS = (DEPTH + N_MIXERS - 1) // N_MIXERS
N_POOL_LAYERS = DEPTH // N_MIXERS
HEAD_DIM = 128
N_HEADS = D_MODEL // HEAD_DIM
N_KV = 8
GROUP = N_HEADS // N_KV
Q_W = N_HEADS * HEAD_DIM
KV_W = N_KV * HEAD_DIM
ATTN_IN_W = 2 * Q_W + 2 * KV_W
WINDOW = 128
BLOCK = 128
ATTN_SCALE = HEAD_DIM ** -0.5
POOL_EXPAND = 2
POOL_W = POOL_EXPAND * D_MODEL
POOL_WINDOWS = (2, 4, 8, 16)
N_POOL_GROUPS = len(POOL_WINDOWS)
POOL_GW = POOL_W // N_POOL_GROUPS
PLE_DIM = 256
EPS = 1e-6

kernel_name = "hybrid_swa_pool_ple_encoder"

def rms_norm(x, g):
    xf = x.astype(jnp.float32)
    y = xf * lax.rsqrt(jnp.mean(xf * xf, axis=-1, keepdims=True) + EPS)
    return (y * g.astype(jnp.float32)).astype(x.dtype)

def alibi_slopes():
    return 2.0 ** (-8.0 * jnp.arange(1, N_HEADS + 1, dtype=jnp.float32) / N_HEADS)

def windowed_gqa(h, w_in, q_g, k_g, sink, w_out):
    B, S, _ = h.shape
    u = h @ w_in
    q, k, v, z = jnp.split(u, [Q_W, Q_W + KV_W, Q_W + 2 * KV_W], axis=-1)
    q = rms_norm(q.reshape(B, S, N_KV, GROUP, HEAD_DIM), q_g)
    k = rms_norm(k.reshape(B, S, N_KV, HEAD_DIM), k_g)
    v = v.reshape(B, S, N_KV, HEAD_DIM)
    nb = S // BLOCK
    pad = ((0, 0), (BLOCK, BLOCK), (0, 0), (0, 0))
    kp = jnp.pad(k, pad)
    vp = jnp.pad(v, pad)
    qb = q.reshape(B, nb, BLOCK, N_KV, GROUP, HEAD_DIM).transpose(1, 0, 2, 3, 4, 5)
    slopes = alibi_slopes().reshape(N_KV, GROUP)
    sink_f = sink.astype(jnp.float32).reshape(N_KV, GROUP)

    def band_block(args):
        qi, bi = args
        kw = lax.dynamic_slice_in_dim(kp, bi * BLOCK, 3 * BLOCK, axis=1)
        vw = lax.dynamic_slice_in_dim(vp, bi * BLOCK, 3 * BLOCK, axis=1)
        s = jnp.einsum('btkgd,bskd->bkgts', qi.astype(jnp.float32),
                       kw.astype(jnp.float32)) * ATTN_SCALE
        t_pos = bi * BLOCK + jnp.arange(BLOCK)
        s_pos = bi * BLOCK - BLOCK + jnp.arange(3 * BLOCK)
        dist = jnp.abs(t_pos[:, None] - s_pos[None, :])
        valid = (dist <= WINDOW) & (s_pos >= 0)[None, :] & (s_pos < S)[None, :]
        s = s - slopes[:, :, None, None] * dist.astype(jnp.float32)
        s = jnp.where(valid, s, -jnp.inf)
        sink_col = jnp.broadcast_to(sink_f[None, :, :, None, None], s.shape[:-1] + (1,))
        pr = jax.nn.softmax(jnp.concatenate([s, sink_col], axis=-1), axis=-1)[..., :-1]
        o = jnp.einsum('bkgts,bskd->btkgd', pr, vw.astype(jnp.float32))
        return o.astype(h.dtype)

    o = lax.map(band_block, (qb, jnp.arange(nb)))
    o = o.transpose(1, 0, 2, 3, 4, 5).reshape(B, S, Q_W)
    return (o * jax.nn.silu(z)) @ w_out

def multiscale_pool(h, w_in, w_grp, scale, w_out):
    B, S, _ = h.shape
    u = h @ w_in
    v, z = jnp.split(u, 2, axis=-1)
    vf = v.astype(jnp.float32)
    c = jnp.pad(jnp.cumsum(vf, axis=1), ((0, 0), (1, 0), (0, 0)))
    t = jnp.arange(S)
    outs = []
    for j, w in enumerate(POOL_WINDOWS):
        left = (w - 1) // 2
        right = w - 1 - left
        lo = jnp.clip(t - left, 0, S)
        hi = jnp.clip(t + right + 1, 0, S)
        cj = c[..., j * POOL_GW:(j + 1) * POOL_GW]
        win_sum = jnp.take(cj, hi, axis=1) - jnp.take(cj, lo, axis=1)
        mean = win_sum / (hi - lo).astype(jnp.float32)[None, :, None]
        outs.append(mean - vf[..., j * POOL_GW:(j + 1) * POOL_GW])
    d = jnp.stack(outs, axis=2).astype(h.dtype)
    y = jnp.einsum('bsgc,gcd->bsgd', d, w_grp).reshape(B, S, POOL_W) * scale
    return (y * jax.nn.silu(z)) @ w_out

def per_layer_embed(x, p_i, norm_g, w_gate, w_proj):
    gate = jax.nn.sigmoid((rms_norm(x, norm_g) @ w_gate).astype(jnp.float32))
    return x + (p_i @ w_proj) * gate.astype(x.dtype)

def setup_inputs(seed: int = 0) -> dict:
    key = jax.random.key(seed)
    ks = jax.random.split(key, 16)
    f32 = jnp.float32
    nrm = lambda k, shape, s: jax.random.normal(k, shape, f32) * s
    return {
        "x": nrm(ks[0], (BATCH, SEQ, D_MODEL), 1.0),
        "p": nrm(ks[1], (DEPTH, BATCH, SEQ, PLE_DIM), 1.0),
        "norm_g": 1.0 + nrm(ks[2], (DEPTH, D_MODEL), 0.02),
        "attn_w_in": nrm(ks[3], (N_ATTN_LAYERS, D_MODEL, ATTN_IN_W), D_MODEL ** -0.5),
        "attn_q_norm_g": 1.0 + nrm(ks[4], (N_ATTN_LAYERS, HEAD_DIM), 0.02),
        "attn_k_norm_g": 1.0 + nrm(ks[5], (N_ATTN_LAYERS, HEAD_DIM), 0.02),
        "attn_sink": nrm(ks[6], (N_ATTN_LAYERS, N_HEADS), 0.5),
        "attn_w_out": nrm(ks[7], (N_ATTN_LAYERS, Q_W, D_MODEL), Q_W ** -0.5),
        "pool_w_in": nrm(ks[8], (N_POOL_LAYERS, D_MODEL, 2 * POOL_W), D_MODEL ** -0.5),
        "pool_w_grp": nrm(ks[9], (N_POOL_LAYERS, N_POOL_GROUPS, POOL_GW, POOL_GW), POOL_GW ** -0.5),
        "pool_scale": 1.0 + nrm(ks[10], (N_POOL_LAYERS, POOL_W), 0.1),
        "pool_w_out": nrm(ks[11], (N_POOL_LAYERS, POOL_W, D_MODEL), POOL_W ** -0.5),
        "ple_norm_g": 1.0 + nrm(ks[12], (DEPTH, D_MODEL), 0.02),
        "ple_w_gate": nrm(ks[13], (DEPTH, D_MODEL, D_MODEL), D_MODEL ** -0.5),
        "ple_w_proj": nrm(ks[14], (DEPTH, PLE_DIM, D_MODEL), PLE_DIM ** -0.5),
    }

def reference(x, p, norm_g, attn_w_in, attn_q_norm_g, attn_k_norm_g, attn_sink,
              attn_w_out, pool_w_in, pool_w_grp, pool_scale, pool_w_out,
              ple_norm_g, ple_w_gate, ple_w_proj):
    for i in range(DEPTH):
        h = rms_norm(x, norm_g[i])
        j = i // N_MIXERS
        if i % N_MIXERS == 0:
            x = x + windowed_gqa(h, attn_w_in[j], attn_q_norm_g[j], attn_k_norm_g[j],
                                 attn_sink[j], attn_w_out[j])
        else:
            x = x + multiscale_pool(h, pool_w_in[j], pool_w_grp[j], pool_scale[j],
                                    pool_w_out[j])
        x = per_layer_embed(x, p[i], ple_norm_g[i], ple_w_gate[i], ple_w_proj[i])
    return x


_drawn_inputs = setup_inputs


def setup_inputs(seed=0):
    import zlib

    import numpy as np

    out = dict(_drawn_inputs(seed))
    spreads = {}
    factors = {'norm_g': 8.0,
     'attn_q_norm_g': 8.0,
     'attn_k_norm_g': 8.0,
     'attn_sink': 5.96,
     'ple_norm_g': 64.0,
     'p': 3.717,
     'ple_w_gate': 5.554,
     'ple_w_proj': 3.706}
    for name, (base, spread) in spreads.items():
        noise = np.random.default_rng([zlib.crc32(name.encode()), seed]).standard_normal(out[name].shape)
        drawn = base * np.exp(spread * noise) if base else spread * noise
        out[name] = __import__('jax').numpy.asarray(drawn.astype(out[name].dtype))
    for name, factor in factors.items():
        out[name] = (out[name] * factor).astype(out[name].dtype)
    return out
```

```python
import concourse.bass as bass
from concourse import mybir
from contextlib import ExitStack

F32 = mybir.dt.float32
F32R = mybir.dt.float32r
I32 = mybir.dt.int32
ALU = mybir.AluOpType
ACT = mybir.ActivationFunctionType
X_AXIS = mybir.AxisListType.X

P = 128
SEQ = 256
D_MODEL = 4096
TOK = SEQ // P
KT = D_MODEL // P
N = 512
HEAD_DIM = 128
N_KV = 8
GROUP = 4
KV_W = N_KV * HEAD_DIM
Q_W = D_MODEL
PLE = 256
PLE_T = PLE // P
EPS = 1e-6
SCALE = HEAD_DIM ** -0.5
WINDOW = 128
MASKED = -1e36

HALVES = KT // 2
SUBS = KT // 4
RING = 4
AHEAD = RING

G_K, G_V, G_Q0 = 0, 2, 4
G_Z = lambda c: 5 + 2 * c
G_OUT = G_Z(N_KV - 1) + 1
G_GATE = G_OUT + D_MODEL // N
CHUNKS = G_GATE + D_MODEL // N
NOUT = D_MODEL // N


def encoder_layer(nc, x, p, norm_g, w_in, q_g, k_g, sink, w_out, ple_g, w_gate, w_proj, out):
    x = x[0]
    p = p[0, 0]
    w_in, w_out, w_gate, w_proj, out = w_in[0], w_out[0], w_gate[0], w_proj[0], out[0]
    ctx = ExitStack()
    with ctx:
        def sb(name, shape, dt=F32):
            return ctx.enter_context(nc.sbuf_tensor(name, shape, dt))

        def sem(name):
            return ctx.enter_context(nc.semaphore(name))

        aT_hi = sb("aT_hi", [P, KT, SEQ], F32R)
        aT_lo = sb("aT_lo", [P, KT, SEQ], F32R)
        stage = sb("stage", [P, KT * SEQ])
        x_in = stage[:, :].rearrange("q (t n) -> q t n", t=TOK)
        nextT = stage[:, :].rearrange("q (j t) -> q j t", t=SEQ)
        raw = sb("raw", [P, RING, 4 * N])
        w_hi = sb("w_hi", [P, RING, 2 * N], F32R)
        w_lo = sb("w_lo", [P, RING, 2 * N], F32R)
        arena = sb("arena", [P, 11776])

        def at(a, size):
            return arena[:, a:a + size]

        kT = at(0, 2048).rearrange("q (h s) -> q h s", h=N_KV)
        v_sb = at(2048, 2048).rearrange("q (t n) -> q t n", t=TOK)
        bias = at(4096, 1536).rearrange("q (h s) -> q h s", h=GROUP)
        qk = at(5632, 1024).rearrange("q (t n) -> q t n", t=TOK)
        S = at(6656, 1024).rearrange("q (h s) -> q h s", h=GROUP)
        PT = at(7680, 1024).rearrange("q (s h t) -> q s h t", s=TOK, h=GROUP)
        qT = at(8704, 1024).rearrange("q (t h n) -> q t h n", t=TOK, h=GROUP)
        sg = at(9728, 1024).rearrange("q (t n) -> q t n", t=TOK)
        o_sb = at(10752, 1024).rearrange("q (t n) -> q t n", t=TOK)
        vecs = at(10752, P)
        dist_i = at(9728, 384).bitcast(I32)
        dist = at(10240, 384)
        squares = at(6656, 1024)
        x1 = at(0, 8192).rearrange("q (t n) -> q t n", t=TOK)
        p_in = at(5632, TOK * PLE).rearrange("q (t n) -> q t n", t=TOK)
        pT = at(8192, 512).rearrange("q (j t) -> q j t", j=PLE_T)
        xres = at(8704, 1024).rearrange("q (t n) -> q t n", t=TOK)
        gate = at(8704, 1024).rearrange("q (t n) -> q t n", t=TOK)
        junk = at(9728, 1024).rearrange("q (t n) -> q t n", t=TOK)
        o_out = at(9728, 1024).rearrange("q (t n) -> q t n", t=TOK)
        wp = at(10752, 1024).rearrange("q (j n) -> q j n", j=PLE_T)

        ident = sb("ident", [P, P])
        NV = 2 * KT + 2
        vecT = sb("vecT", [P, NV])
        g1T, g2T, qgT, kgT = vecT[:, 0:KT], vecT[:, KT:2 * KT], vecT[:, 2 * KT:2 * KT + 1], vecT[:, 2 * KT + 1:NV]
        nsink = sb("nsink", [P, N_KV * GROUP])
        ss0 = sb("ss0", [P, TOK, 4])
        ss1 = sb("ss1", [P, TOK, NOUT])
        ssr = sb("ssr", [P, TOK])
        r = sb("r", [P, TOK])
        mhalf = sb("mhalf", [P, TOK * GROUP])
        half = sb("half", [P, GROUP])
        ssq = sb("ssq", [P, TOK * GROUP])
        rstd = sb("rstd", [P, TOK, GROUP])
        nm = sb("nm", [P, TOK, GROUP])
        sd = sb("sd", [P, TOK, GROUP])
        den = sb("den", [P, TOK, GROUP])
        rinv = sb("rinv", [P, TOK, GROUP])

        bank = [ctx.enter_context(nc.psum_tensor(f"bank{i}", [P, N], F32)) for i in range(8)]
        acc = [bank[0:2], bank[2:4]]

        raw_in = [sem(f"raw_in{i}") for i in range(RING)]
        hi_done, lo_done = sem("hi_done"), sem("lo_done")
        pe_half = sem("pe_half")
        acc_free = sem("acc_free")
        gate_read = sem("gate_read")
        x_landed = [sem(f"x_landed{i}") for i in range(4)]
        vec_landed, sink_landed = sem("vec_landed"), sem("sink_landed")
        ident_zero, ident_ready = sem("ident_zero"), sem("ident_ready")
        iota_ready, dist_f, dist_neg = sem("iota_ready"), sem("dist_f"), sem("dist_neg")
        dist_mask, bias_ready = sem("dist_mask"), sem("bias_ready")
        exponent_ready = sem("exponent_ready")
        vec_tp, vec_ready, nsink_ready = sem("vec_tp"), sem("vec_ready"), sem("nsink_ready")
        xT_ps, xT_hi, xT_lo = sem("xT_ps"), sem("xT_hi"), sem("xT_lo")
        ss0_part, ss_sum, mean_ready, r_ready = sem("ss0_part"), sem("ss_sum"), sem("mean_ready"), sem("r_ready")
        qk_sb, qk_sq, qk_ss, qk_mean, qk_rstd = (sem("qk_sb"), sem("qk_sq"), sem("qk_ss"), sem("qk_mean"),
                                                 sem("qk_rstd"))
        k_normed, qk_tp, qk_T = sem("k_normed"), sem("qk_tp"), sem("qk_T")
        scores_ps, scores_sb, rowmax, max_ready = (sem("scores_ps"), sem("scores_sb"), sem("rowmax"),
                                                   sem("max_ready"))
        sink_diff, probs_ready, probs_tp, probs_T = (sem("sink_diff"), sem("probs_ready"), sem("probs_tp"),
                                                     sem("probs_T"))
        den_sum, rinv_ready, o_ps, o_ready = sem("den_sum"), sem("rinv_ready"), sem("o_ps"), sem("o_ready")
        sg_ready, sz_ready, go_ready, go_tp, go_T = (sem("sg_ready"), sem("sz_ready"), sem("go_ready"),
                                                     sem("go_tp"), sem("go_T"))
        conv_hi, conv_lo = sem("conv_hi"), sem("conv_lo")
        xres_in, x1_kept, x1_tp, x1_T, x1_sq = (sem("xres_in"), sem("x1_kept"), sem("x1_tp"), sem("x1_T"),
                                                sem("x1_sq"))
        p_landed, p_tp, p_T = sem("p_landed"), sem("p_tp"), sem("p_T")
        wp_in, proj_ps, gate_ready, gated_proj, out_ready, out_stored = (
            sem("wp_in"), sem("proj_ps"), sem("gate_ready"), sem("gated_proj"), sem("out_ready"),
            sem("out_stored"))

        block = ctx.enter_context(nc.Block())

        @block.sync
        def _(sp):
            def chunk(g, w, col):
                for u in range(SUBS):
                    if not (isinstance(g, int) and g == 0 and u < RING):
                        sp.wait_ge(lo_done, g * HALVES + 2 * (u - RING + 1))
                    src = w[4 * P * u:4 * P * (u + 1), bass.ds(col, N)].rearrange("(a q) n -> q a n", q=P)
                    dst = raw[:, u % RING, :].rearrange("q (a n) -> q a n", a=4)
                    sp.dma_start(dst, src).then_inc(raw_in[u % RING], 16)

            chunk(0, w_in, Q_W)
            with sp.Fori(1, G_Q0) as g:
                chunk(g, w_in, g * N + Q_W)
            chunk(G_Q0, w_in, 0)
            with sp.Fori(0, N_KV - 1) as c:
                chunk(c * 2 + G_Z(0), w_in, c * N + (Q_W + 2 * KV_W))
                chunk(c * 2 + (G_Z(0) + 1), w_in, c * N + N)
            chunk(G_Z(N_KV - 1), w_in, Q_W + 2 * KV_W + (N_KV - 1) * N)
            with sp.Fori(0, NOUT) as n:
                chunk(n + G_OUT, w_out, n * N)
            with sp.Fori(0, NOUT) as n:
                chunk(n + G_GATE, w_gate, n * N)

        @block.gpsimd
        def _(pool):
            pool.memset(ident[:, :], 0.0).then_inc(ident_zero, 1)
            pool.wait_ge(ident_zero, 1)
            pool.affine_select(out=ident[:, :], in_=ident[:, :], compare_op=ALU.not_equal, fill=1.0, base=0,
                               pattern=[[-1, P]], channel_multiplier=1).then_inc(ident_ready, 1)
            pool.memset(half[:, :], 0.5).then_inc(exponent_ready, 1)
            pool.memset(mhalf[:, :], -0.5).then_inc(exponent_ready, 1)
            pool.iota(dist_i, pattern=[[-1, 3 * P]], base=P, channel_multiplier=1).then_inc(iota_ready, 1)
            pool.wait_ge(dist_neg, 1)
            pool.affine_select(out=dist, in_=dist, compare_op=ALU.is_ge, fill=MASKED, base=P + WINDOW,
                               pattern=[[-1, 3 * P]], channel_multiplier=1).then_inc(dist_mask, 1)
            pool.wait_ge(dist_mask, 1)
            pool.affine_select(out=dist, in_=dist, compare_op=ALU.is_ge, fill=MASKED, base=WINDOW - P,
                               pattern=[[1, 3 * P]], channel_multiplier=-1).then_inc(dist_mask, 1)
            pool.wait_ge(dist_mask, 2)
            for h in range(GROUP):
                last = pool.tensor_scalar(bias[:, h, :], dist, 2.0 ** (-8.0 * (h + 1) / (N_KV * GROUP)), None,
                                          ALU.mult)
            last.then_inc(bias_ready, 1)
            pool.wait_ge(exponent_ready, 2)

            rstd_flat = rstd[:, :, :].rearrange("q t h -> q (t h)")
            pool.wait_ge(mean_ready, 1)
            pool.tensor_tensor(r[:, :], ssr[:, :], mhalf[:, 0:TOK], ALU.pow).then_inc(r_ready, 1)
            for e in range(2):
                pool.wait_ge(qk_mean, e + 1)
                pool.tensor_tensor(rstd_flat, ssq[:, :], mhalf[:, :], ALU.pow).then_inc(qk_rstd, 1)

            def group(c):
                pool.wait_ge(qk_mean, c + 3)
                pool.tensor_tensor(rstd_flat, ssq[:, :], mhalf[:, :], ALU.pow).then_inc(qk_rstd, 1)

            with pool.Fori(0, N_KV - 1) as c:
                group(c)
                pool.wait_ge(scores_sb, c * 2 + 2)
                pool.tensor_tensor(bias, bias, half[:, :].unsqueeze(2).to_broadcast([P, GROUP, 3 * P]), ALU.mult)\
                    .then_inc(bias_ready, 1)
            group(N_KV - 1)
            with pool.Fori(0, NOUT) as n:
                pool.wait_ge(acc_free, n + (G_OUT + 1))
                pool.tensor_copy(x1[:, :, bass.ds(n * N, N)], xres).then_inc(x1_kept, 1)
            pool.wait_ge(mean_ready, 2)
            pool.tensor_tensor(r[:, :], ssr[:, :], mhalf[:, 0:TOK], ALU.pow).then_inc(r_ready, 1)

        @block.scalar
        def _(act):
            def hi_half(g, i):
                load = i // 2
                act.wait_ge(raw_in[load % RING], g * 32 + 16 * (load // RING + 1))
                if not (isinstance(g, int) and g == 0 and i < RING):
                    act.wait_ge(pe_half, g * HALVES + (i - RING + 1))
                nc.scalar.activation(w_hi[:, i % RING, :], raw[:, load % RING, (i % 2) * 2 * N:(i % 2 + 1) * 2 * N],
                                     ACT.Copy).then_inc(hi_done, 1)

            for k in range(4):
                cols = slice(k * 1024, (k + 1) * 1024)
                act.dma_start(x_in[:, :, cols], x[:, cols].rearrange("(t q) n -> q t n", q=P))\
                   .then_inc(x_landed[k], 16)
                if k == 0:
                    for row, src in ((0, norm_g), (KT, ple_g)):
                        act.dma_start(vecs[row:row + KT, :], src[0, :].rearrange("(j q) -> j q", q=P))\
                           .then_inc(vec_landed, 16)
                    for row, src in ((2 * KT, q_g), (2 * KT + 1, k_g)):
                        act.dma_start(vecs[row:row + 1, :], src[0:1, :]).then_inc(vec_landed, 16)
            act.dma_start(nsink[:, :], sink[0, :].partition_broadcast(P)).then_inc(sink_landed, 16)

            def xT_hi_pair(i):
                act.wait_ge(xT_ps, i + 1)
                for jj in range(2):
                    j = 2 * i + jj
                    last = nc.scalar.activation(aT_hi[:, j, :], bank[4 + i % 4][:, jj * SEQ:(jj + 1) * SEQ],
                                                ACT.Copy, scale=g1T[:, j:j + 1])
                last.then_inc(xT_hi, 1)

            def qk_transposed(e, gvec, dsts):
                act.wait_ge(qk_tp, e + 1)
                for t in range(TOK):
                    last = nc.scalar.activation(dsts[t], bank[4 + t][:, :].rearrange("q (h n) -> q h n", h=GROUP),
                                                ACT.Copy, scale=gvec)
                last.then_inc(qk_T, 1)

            def exps(c, b):
                act.wait_ge(max_ready, c * 2 + (b + 1))
                for h in range(GROUP):
                    nc.scalar.activation(S[:, h, :], S[:, h, :], ACT.Exp, bias=nm[:, b, h:h + 1],
                                         accum_out=den[:, b, h:h + 1])
                nc.scalar.activation(sd[:, b, :], sd[:, b, :], ACT.Exp).then_inc(probs_ready, 1)

            def probs_transposed(c, b):
                act.wait_ge(probs_tp, c * 2 + (b + 1))
                for s in range(TOK):
                    last = nc.scalar.activation(PT[:, s, :, :].rearrange("q h t -> q (h t)"), bank[4 + s][:, :],
                                                ACT.Copy)
                last.then_inc(probs_T, 1)

            def z_sigmoid(c):
                act.wait_ge(pe_half, (c * 2 + (G_Z(0) + 1)) * HALVES)
                for t in range(TOK):
                    last = nc.scalar.activation(sg[:, t, :], acc[1][t][:, :], ACT.Sigmoid, scale=r[:, t:t + 1])
                last.then_inc(sg_ready, 1)

            def gated_transposed(c):
                act.wait_ge(go_tp, c + 1)
                for jj in range(2):
                    last = nc.scalar.activation(nextT[:, bass.ds(c * 4 + 2 * jj, 2), :],
                                                bank[4 + jj][:, :].rearrange("q (j t) -> q j t", j=2), ACT.Copy)
                last.then_inc(go_T, 1)

            def convert_hi(phase, i, g_before, written, count):
                act.wait_ge(pe_half, g_before * HALVES + i + 1)
                act.wait_ge(written, count)
                nc.scalar.activation(aT_hi[:, 2 * i:2 * i + 2, :], nextT[:, 2 * i:2 * i + 2, :], ACT.Copy)\
                  .then_inc(conv_hi, 1)

            def x1_transposed(n):
                act.wait_ge(x1_tp, n + 1)
                for jj in range(4):
                    b = bank[4 + jj // 2][:, (jj % 2) * SEQ:(jj % 2 + 1) * SEQ]
                    last = nc.scalar.activation(nextT[:, bass.ds(n * 4 + jj, 1), :].rearrange("q a t -> q (a t)"), b,
                                                ACT.Copy, scale=g2T[:, bass.ds(n * 4 + jj, 1)])
                last.then_inc(x1_T, 1)

            def x1_squares(n):
                act.wait_ge(acc_free, n + (G_OUT + 1))
                for t in range(TOK):
                    last = nc.scalar.activation(junk[:, t, :], xres[:, t, :], ACT.Square,
                                                accum_out=ss1[:, t, bass.ds(n, 1)])
                last.then_inc(x1_sq, 1)

            def load_residual(n):
                if not (isinstance(n, int) and n == 0):
                    act.wait_ge(x1_sq, n)
                    act.wait_ge(x1_kept, n)
                act.dma_start(xres, x[:, bass.ds(n * N, N)].rearrange("(t q) n -> q t n", q=P)).then_inc(xres_in, 16)

            def load_proj(n):
                act.dma_start(wp, w_proj[:, bass.ds(n * N, N)].rearrange("(j q) n -> q j n", q=P)).then_inc(wp_in, 16)

            def gate_sigmoid(n, pair):
                act.wait_ge(pe_half, (n + (G_GATE + 1)) * HALVES)
                for t in range(TOK):
                    last = nc.scalar.activation(gate[:, t, :], acc[pair][t][:, :], ACT.Sigmoid, scale=r[:, t:t + 1])
                last.then_inc(gate_read, 1)

            def store(n):
                act.wait_ge(out_ready, n + 1)
                act.dma_start(out[:, bass.ds(n * N, N)].rearrange("(t q) n -> q t n", q=P), o_out)\
                   .then_inc(out_stored, 16)

            act.wait_ge(vec_tp, 1)
            nc.scalar.activation(vecT[:, :], bank[7][:, 0:NV], ACT.Copy).then_inc(vec_ready, 1)
            act.wait_ge(vec_ready, 1)
            for i in range(HALVES):
                xT_hi_pair(i)
                hi_half(0, i)
            for g in (1, 2, 3, 4):
                for i in range(HALVES):
                    hi_half(g, i)
                    if i == 7 and g <= 2:
                        e = g - 1
                        qk_transposed(e, kgT, [kT[:, 4 * e:4 * e + 4, t * P:(t + 1) * P] for t in range(TOK)])

            def attention(c, i):
                if i == 5:
                    qk_transposed(c + 2, qgT, [qT[:, t] for t in range(TOK)])
                elif i == 8:
                    exps(c, 0)
                elif i == 11:
                    probs_transposed(c, 0)
                elif i == 13:
                    exps(c, 1)

            def gating(c, i):
                if i == 0:
                    probs_transposed(c, 1)
                elif i == 2:
                    z_sigmoid(c)
                elif i == 6:
                    gated_transposed(c)

            with act.Fori(0, N_KV - 1) as c:
                for i in range(HALVES):
                    hi_half(c * 2 + G_Z(0), i)
                    attention(c, i)
                for i in range(HALVES):
                    hi_half(c * 2 + (G_Z(0) + 1), i)
                    gating(c, i)

            c = N_KV - 1
            for i in range(HALVES):
                hi_half(G_Z(c), i)
                attention(c, i)
                if i >= AHEAD:
                    convert_hi(0, i - AHEAD, G_Z(c), go_T, (i - AHEAD) // 2 + 1)
            for i in range(HALVES):
                hi_half(G_OUT, i)
                if i == 0:
                    act.wait_ge(qk_tp, c + 3)
                    act.wait_ge(qk_ss, c + 3)
                    act.dma_start(p_in, p.rearrange("(t q) n -> q t n", q=P)).then_inc(p_landed, 16)
                gating(c, i)
                if i < 2:
                    convert_hi(0, 12 + i, G_Z(c), go_T, (12 + i) // 2 + 1)
                elif i in (8, 9):
                    convert_hi(0, 6 + i, G_Z(c), go_T, N_KV)
                elif i == 10:
                    act.wait_ge(scores_ps, 2 * N_KV)
                    load_residual(0)
                elif i == 11:
                    act.wait_ge(p_tp, 1)
                    nc.scalar.activation(pT.rearrange("q j t -> q (j t)"), bank[6][:, :], ACT.Copy).then_inc(p_T, 1)

            def out_chunk(n):
                for i in range(HALVES):
                    hi_half(n + G_OUT, i)
                    if i == 5:
                        x1_transposed(n - 1)
                    elif i == 7:
                        x1_squares(n - 1)
                    elif i == 9:
                        load_residual(n)

            act.wait_ge(conv_lo, HALVES)
            act.wait_ge(go_ready, N_KV)
            with act.Fori(1, NOUT - 1) as n:
                out_chunk(n)
            n = NOUT - 1
            for i in range(HALVES):
                hi_half(n + G_OUT, i)
                if i == 5:
                    x1_transposed(n - 1)
                elif i == 7:
                    x1_squares(n - 1)
                elif i == 9:
                    load_residual(n)
                elif i == 10:
                    load_proj(0)
                if i >= AHEAD:
                    convert_hi(1, i - AHEAD, G_GATE - 1, x1_T, (i - AHEAD) // 2 + 1)
            for i in range(HALVES):
                hi_half(G_GATE, i)
                if i < 2:
                    convert_hi(1, 12 + i, G_GATE - 1, x1_T, (12 + i) // 2 + 1)
                elif i == 5:
                    x1_transposed(NOUT - 1)
                elif i == 7:
                    x1_squares(NOUT - 1)
                elif i in (8, 9):
                    convert_hi(1, 6 + i, G_GATE - 1, x1_T, NOUT)
                elif i == 15:
                    act.wait_ge(proj_ps, 1)
                    load_proj(1)

            def gate_chunk(n, pair, more):
                for i in range(HALVES):
                    hi_half(n + G_GATE, i)
                    if i == 2:
                        gate_sigmoid(n - 1, pair)
                    elif i == 8:
                        store(n - 1)
                    elif i == 15 and more:
                        act.wait_ge(proj_ps, n + 1)
                        load_proj(n + 1)

            act.wait_ge(r_ready, 2)
            with act.Fori(0, NOUT // 2 - 1) as m:
                n = m * 2 + 1
                gate_chunk(n, 0, True)
                gate_chunk(n + 1, 1, True)
            gate_chunk(NOUT - 1, 0, False)
            gate_sigmoid(NOUT - 1, 1)
            store(NOUT - 1)
            act.wait_ge(out_stored, 16 * NOUT)

        @block.vector
        def _(dve):
            def lo_half(g, i):
                dve.wait_ge(hi_done, g * HALVES + (i + 1))
                load = i // 2
                nc.vector.tensor_tensor(w_lo[:, i % RING, :],
                                        raw[:, load % RING, (i % 2) * 2 * N:(i % 2 + 1) * 2 * N],
                                        w_hi[:, i % RING, :].bitcast(F32), ALU.subtract).then_inc(lo_done, 1)

            dve.wait_ge(iota_ready, 1)
            nc.vector.tensor_copy(dist, dist_i).then_inc(dist_f, 1)
            dve.wait_ge(dist_f, 1)
            nc.vector.scalar_tensor_tensor(dist, dist, -1.0, dist, ALU.mult, ALU.min).then_inc(dist_neg, 1)
            dve.wait_ge(sink_landed, 16)
            nc.vector.tensor_scalar(nsink[:, :], nsink[:, :], -1.0, None, ALU.mult).then_inc(nsink_ready, 1)
            dve.wait_ge(vec_ready, 1)

            for i in range(HALVES):
                dve.wait_ge(xT_hi, i + 1)
                for jj in range(2):
                    j = 2 * i + jj
                    last = nc.vector.scalar_tensor_tensor(aT_lo[:, j, :], bank[4 + i % 4][:, jj * SEQ:(jj + 1) * SEQ],
                                                          g1T[:, j:j + 1], aT_hi[:, j, :].bitcast(F32), ALU.mult,
                                                          ALU.subtract)
                last.then_inc(xT_lo, 1)
                lo_half(0, i)
                if i % 2 == 1:
                    t, k = (i // 2) % 2, i // 4
                    dve.wait_ge(x_landed[k], 16)
                    if i > 1:
                        dve.wait_ge(ss0_part, i // 2)
                    xs = x_in[:, t, k * 1024:(k + 1) * 1024]
                    nc.vector.scalar_tensor_tensor(squares, xs, 1.0, xs, ALU.mult, ALU.mult,
                                                   accum_out=ss0[:, t, k:k + 1]).then_inc(ss0_part, 1)
            dve.wait_ge(ss0_part, 8)
            nc.vector.tensor_reduce(ssr[:, :], ss0[:, :, :], X_AXIS, ALU.add).then_inc(ss_sum, 1)
            dve.wait_ge(ss_sum, 1)
            nc.vector.tensor_scalar(ssr[:, :], ssr[:, :], 1.0 / D_MODEL, EPS, ALU.mult, ALU.add)\
              .then_inc(mean_ready, 1)

            def evacuate(g, pair, dsts):
                dve.wait_ge(pe_half, g * HALVES + HALVES)
                for t in range(TOK):
                    last = nc.vector.tensor_scalar(dsts[t], acc[pair][t][:, :], r[:, t:t + 1], None, ALU.mult)
                last.then_inc(acc_free, 1)

            def qk_squares(g):
                dve.wait_ge(acc_free, g + 1)
                flat = qk.rearrange("q t n -> q (t n)")
                nc.vector.tensor_tensor(squares, flat, flat, ALU.mult).then_inc(qk_sq, 1)

            def qk_sums(e, scale=1.0):
                dve.wait_ge(qk_sq, e + 1)
                nc.vector.tensor_reduce(ssq[:, :], squares.rearrange("q (h n) -> q h n", n=HEAD_DIM), X_AXIS,
                                        ALU.add).then_inc(qk_ss, 1)
                dve.wait_ge(qk_ss, e + 1)
                nc.vector.tensor_scalar(ssq[:, :], ssq[:, :], 1.0 / (HEAD_DIM * scale ** 2), EPS / scale ** 2, ALU.mult,
                                        ALU.add)\
                  .then_inc(qk_mean, 1)

            dve.wait_ge(r_ready, 1)
            for g in (1, 2, 3, 4):
                for i in range(HALVES):
                    lo_half(g, i)
                    e = g - 1
                    if i == 2 and g <= 2:
                        evacuate(e, e % 2, [qk[:, t, :] for t in range(TOK)])
                    elif i == 2:
                        evacuate(e, e % 2, [v_sb[:, t, (e - 2) * N:(e - 1) * N] for t in range(TOK)])
                    elif i == 3 and g <= 2:
                        qk_squares(e)
                        qk_sums(e)
                    elif i == 5 and g <= 2:
                        dve.wait_ge(qk_rstd, e + 1)
                        nc.vector.tensor_tensor(
                            qk.rearrange("q t (h n) -> q (t h) n", n=HEAD_DIM),
                            qk.rearrange("q t (h n) -> q (t h) n", n=HEAD_DIM),
                            rstd[:, :, :].rearrange("q t h -> q (t h)").unsqueeze(2)
                                .to_broadcast([P, TOK * GROUP, HEAD_DIM]), ALU.mult).then_inc(k_normed, 1)

            def score_rows(c, b):
                dve.wait_ge(scores_ps, c * 2 + (b + 1))
                if b == 0:
                    dve.wait_ge(bias_ready, c + 1)
                    dve.wait_ge(qk_rstd, c + 3)
                else:
                    dve.wait_ge(probs_tp, c * 2 + 1)
                for h in range(GROUP):
                    ps = bank[6 + h // 2][:, (h % 2) * SEQ:(h % 2 + 1) * SEQ]
                    last = nc.vector.scalar_tensor_tensor(S[:, h, :], ps, rstd[:, b, h:h + 1],
                                                          bias[:, h, P * (1 - b):P * (1 - b) + SEQ], ALU.mult, ALU.add)
                last.then_inc(scores_sb, 1)

            def maxima(c, b):
                k = c * 2 + (b + 1)
                dve.wait_ge(scores_sb, k)
                nc.vector.tensor_reduce(nm[:, b, :], S, X_AXIS, ALU.max, negate=True).then_inc(rowmax, 1)
                dve.wait_ge(rowmax, k)
                sinks = nsink[:, bass.ds(c * GROUP, GROUP)]
                nc.vector.tensor_tensor(nm[:, b, :], nm[:, b, :], sinks, ALU.min).then_inc(sink_diff, 1)
                dve.wait_ge(sink_diff, k)
                nc.vector.tensor_tensor(sd[:, b, :], nm[:, b, :], sinks, ALU.subtract).then_inc(max_ready, 1)

            def head_outputs(c, b):
                k = c * 2 + (b + 1)
                dve.wait_ge(probs_ready, k)
                nc.vector.tensor_tensor(den[:, b, :], den[:, b, :], sd[:, b, :], ALU.add).then_inc(den_sum, 1)
                dve.wait_ge(den_sum, k)
                nc.vector.reciprocal(rinv[:, b, :], den[:, b, :]).then_inc(rinv_ready, 1)
                dve.wait_ge(rinv_ready, k)
                dve.wait_ge(o_ps, k)
                nc.vector.tensor_tensor(o_sb[:, b, :].rearrange("q (h n) -> q h n", h=GROUP),
                                        bank[4][:, :].rearrange("q (h n) -> q h n", h=GROUP),
                                        rinv[:, b, :].unsqueeze(2).to_broadcast([P, GROUP, HEAD_DIM]), ALU.mult)\
                  .then_inc(o_ready, 1)

            def attention(c, i):
                g = c * 2 + G_Z(0)
                if i == 2:
                    evacuate(g - 1, 0, [qk[:, t, :] for t in range(TOK)])
                elif i == 3:
                    qk_squares(g - 1)
                elif i == 4:
                    qk_sums(c + 2, SCALE)
                elif i == 7:
                    score_rows(c, 0)
                elif i == 8:
                    maxima(c, 0)
                elif i == 11:
                    score_rows(c, 1)
                elif i == 12:
                    maxima(c, 1)
                elif i == 13:
                    head_outputs(c, 0)

            def gating(c, i):
                if i == 2:
                    head_outputs(c, 1)
                elif i == 3:
                    dve.wait_ge(sg_ready, c + 1)
                    for t in range(TOK):
                        last = nc.vector.scalar_tensor_tensor(sg[:, t, :], acc[1][t][:, :], r[:, t:t + 1], sg[:, t, :],
                                                              ALU.mult, ALU.mult)
                    last.then_inc(acc_free, 1)
                elif i == 4:
                    dve.wait_ge(acc_free, c * 2 + (G_Z(0) + 1))
                    dve.wait_ge(o_ready, c * 2 + 2)
                    nc.vector.tensor_tensor(o_sb, o_sb, sg, ALU.mult).then_inc(go_ready, 1)

            def convert_lo(k, i):
                dve.wait_ge(conv_hi, k)
                nc.vector.tensor_tensor(aT_lo[:, 2 * i:2 * i + 2, :], nextT[:, 2 * i:2 * i + 2, :],
                                        aT_hi[:, 2 * i:2 * i + 2, :].bitcast(F32), ALU.subtract).then_inc(conv_lo, 1)

            with dve.Fori(0, N_KV - 1) as c:
                for i in range(HALVES):
                    lo_half(c * 2 + G_Z(0), i)
                    attention(c, i)
                for i in range(HALVES):
                    lo_half(c * 2 + (G_Z(0) + 1), i)
                    gating(c, i)
            c = N_KV - 1
            for i in range(HALVES):
                lo_half(G_Z(c), i)
                attention(c, i)
                if i >= AHEAD:
                    convert_lo(i - AHEAD + 1, i - AHEAD)
            for i in range(HALVES):
                lo_half(G_OUT, i)
                gating(c, i)
                if i < 2:
                    convert_lo(13 + i, 12 + i)
                elif i in (8, 9):
                    convert_lo(7 + i, 6 + i)

            def residual(n, pair):
                dve.wait_ge(pe_half, (n + (G_OUT + 1)) * HALVES)
                dve.wait_ge(xres_in, n * 16 + 16)
                for t in range(TOK):
                    last = nc.vector.tensor_tensor(xres[:, t, :], acc[pair][t][:, :], xres[:, t, :], ALU.add)
                last.then_inc(acc_free, 1)

            with dve.Fori(0, NOUT // 2 - 1) as m:
                n = m * 2 + 1
                for k in range(2):
                    for i in range(HALVES):
                        lo_half(n + (G_OUT + k), i)
                        if i == 2:
                            residual(n + (k - 1), k)
            for i in range(HALVES):
                lo_half(G_OUT + NOUT - 1, i)
                if i == 2:
                    residual(NOUT - 2, 0)
                if i >= AHEAD:
                    convert_lo(HALVES + i - AHEAD + 1, i - AHEAD)
            for i in range(HALVES):
                lo_half(G_GATE, i)
                if i < 2:
                    convert_lo(HALVES + 13 + i, 12 + i)
                if i == 2:
                    residual(NOUT - 1, 1)
                elif i == 9:
                    dve.wait_ge(x1_sq, NOUT)
                    nc.vector.tensor_reduce(ssr[:, :], ss1[:, :, :], X_AXIS, ALU.add).then_inc(ss_sum, 1)
                    dve.wait_ge(ss_sum, 2)
                    nc.vector.tensor_scalar(ssr[:, :], ssr[:, :], 1.0 / D_MODEL, EPS, ALU.mult, ALU.add)\
                      .then_inc(mean_ready, 1)
                if i in (8, 9):
                    convert_lo(HALVES + 7 + i, 6 + i)

            def gate_proj(n):
                dve.wait_ge(gate_read, n + 1)
                dve.wait_ge(proj_ps, n + 1)
                if not (isinstance(n, int) and n == 0):
                    dve.wait_ge(out_stored, n * 16)
                for t in range(TOK):
                    last = nc.vector.tensor_tensor(o_out[:, t, :], bank[6 + t][:, :], gate[:, t, :], ALU.mult)
                last.then_inc(gated_proj, 1)

            def add_x1(n):
                dve.wait_ge(gated_proj, n + 1)
                nc.vector.tensor_tensor(o_out, o_out, x1[:, :, bass.ds(n * N, N)], ALU.add).then_inc(out_ready, 1)

            dve.wait_ge(x1_kept, NOUT)

            def gate_chunk(n):
                for i in range(HALVES):
                    lo_half(n + G_GATE, i)
                    if i == 4:
                        gate_proj(n - 1)
                    elif i == 5:
                        add_x1(n - 1)

            gate_chunk(1)
            with dve.Fori(2, NOUT) as n:
                gate_chunk(n)
            gate_proj(NOUT - 1)
            add_x1(NOUT - 1)

        @block.tensor
        def _(pe):
            def half(g, i, pair):
                pe.wait_ge(lo_done, g * HALVES + (i + 1))
                for jj in range(2):
                    j = 2 * i + jj
                    whi = w_hi[:, i % RING, jj * N:(jj + 1) * N]
                    wlo = w_lo[:, i % RING, jj * N:(jj + 1) * N]
                    for t in range(TOK):
                        ahi = aT_hi[:, j, t * P:(t + 1) * P]
                        alo = aT_lo[:, j, t * P:(t + 1) * P]
                        nc.tensor.matmul(acc[pair][t][:, :], ahi, wlo, start=(j == 0), stop=False)
                        nc.tensor.matmul(acc[pair][t][:, :], ahi, whi, start=False, stop=False)
                        last = nc.tensor.matmul(acc[pair][t][:, :], alo, whi, start=False, stop=(j == KT - 1))
                last.then_inc(pe_half, 1)

            def transpose_tokens(src, banks, done):
                for t in range(TOK):
                    for h in range(GROUP):
                        last = nc.tensor.transpose(banks[t][:, h * P:(h + 1) * P], src[:, t, h * P:(h + 1) * P],
                                                   ident[:, :])
                last.then_inc(done, 1)

            def transpose_columns(src, banks, done):
                for j in range(4):
                    for t in range(TOK):
                        last = nc.tensor.transpose(banks[j // 2][:, (j % 2) * SEQ + t * P:(j % 2) * SEQ + (t + 1) * P],
                                                   src[:, t, j * P:(j + 1) * P], ident[:, :])
                last.then_inc(done, 1)

            def x_pair(i):
                if i % 4 == 0:
                    pe.wait_ge(x_landed[i // 4], 16)
                if i == 3:
                    pe.wait_ge(vec_ready, 1)
                if i >= 4:
                    pe.wait_ge(xT_lo, i - 3)
                for jj in range(2):
                    j = 2 * i + jj
                    for t in range(TOK):
                        last = nc.tensor.transpose(bank[4 + i % 4][:, jj * SEQ + t * P:jj * SEQ + (t + 1) * P],
                                                   x_in[:, t, j * P:(j + 1) * P], ident[:, :])
                last.then_inc(xT_ps, 1)

            pe.wait_ge(ident_ready, 1)
            pe.wait_ge(vec_landed, 64)
            nc.tensor.transpose(bank[7][:, 0:NV], vecs[0:NV, :], ident[0:NV, 0:NV]).then_inc(vec_tp, 1)
            for i in range(4):
                x_pair(i)
            for i in range(HALVES):
                pe.wait_ge(xT_lo, i + 1)
                half(0, i, 0)
                if i + 4 < HALVES:
                    x_pair(i + 4)

            for g in (1, 2, 3, 4):
                if g >= 2:
                    pe.wait_ge(acc_free, g - 1)
                for i in range(HALVES):
                    half(g, i, g % 2)
                    if i == 4 and g <= 2:
                        pe.wait_ge(k_normed, g)
                        if g == 2:
                            pe.wait_ge(qk_T, 1)
                        transpose_tokens(qk, bank[4:6], qk_tp)

            def scores(c, b):
                if b == 0:
                    pe.wait_ge(qk_T, c + 3)
                else:
                    pe.wait_ge(scores_sb, c * 2 + 1)
                for h in range(GROUP):
                    last = nc.tensor.matmul(bank[6 + h // 2][:, (h % 2) * SEQ:(h % 2 + 1) * SEQ], qT[:, b, h, :],
                                            kT[:, bass.ds(c, 1), :].rearrange("q a s -> q (a s)"),
                                            start=True, stop=True)
                last.then_inc(scores_ps, 1)

            def transpose_probs(c, b):
                pe.wait_ge(probs_ready, c * 2 + (b + 1))
                if b == 1:
                    pe.wait_ge(o_ready, c * 2 + 1)
                for s in range(TOK):
                    for h in range(GROUP):
                        last = nc.tensor.transpose(bank[4 + s][:, h * P:(h + 1) * P], S[:, h, s * P:(s + 1) * P],
                                                   ident[:, :])
                last.then_inc(probs_tp, 1)

            def head_values(c, b):
                pe.wait_ge(probs_T, c * 2 + (b + 1))
                for h in range(GROUP):
                    for s in range(TOK):
                        last = nc.tensor.matmul(bank[4][:, h * P:(h + 1) * P], PT[:, s, h, :],
                                                v_sb[:, s, bass.ds(c * HEAD_DIM, HEAD_DIM)],
                                                start=(s == 0), stop=(s == TOK - 1))
                last.then_inc(o_ps, 1)

            def attention(c, i):
                if i == 1:
                    pe.wait_ge(acc_free, c * 2 + G_Z(0))
                    transpose_tokens(qk, bank[4:6], qk_tp)
                elif i == 4:
                    scores(c, 0)
                elif i == 7:
                    scores(c, 1)
                elif i == 8:
                    transpose_probs(c, 0)
                elif i == 10:
                    head_values(c, 0)
                elif i == 13:
                    transpose_probs(c, 1)
                elif i == 15:
                    head_values(c, 1)

            def gating(c, i):
                if i == 4:
                    pe.wait_ge(go_ready, c + 1)
                    transpose_columns(o_sb, bank[4:6], go_tp)

            with pe.Fori(0, N_KV - 1) as c:
                g = c * 2 + G_Z(0)
                pe.wait_ge(acc_free, g - 1)
                for i in range(HALVES):
                    half(g, i, 1)
                    attention(c, i)
                pe.wait_ge(acc_free, g)
                for i in range(HALVES):
                    half(g + 1, i, 0)
                    gating(c, i)
            c = N_KV - 1
            pe.wait_ge(acc_free, G_Z(c) - 1)
            for i in range(HALVES):
                half(G_Z(c), i, 1)
                attention(c, i)
            pe.wait_ge(acc_free, G_OUT - 1)
            for i in range(HALVES):
                pe.wait_ge(conv_lo, i + 1)
                half(G_OUT, i, 0)
                gating(c, i)
                if i == 8:
                    pe.wait_ge(p_landed, 16)
                    for j in range(PLE_T):
                        for t in range(TOK):
                            last = nc.tensor.transpose(bank[6][:, j * SEQ + t * P:j * SEQ + (t + 1) * P],
                                                       p_in[:, t, j * P:(j + 1) * P], ident[:, :])
                    last.then_inc(p_tp, 1)

            def x1_transpose(n):
                pe.wait_ge(acc_free, n + (G_OUT + 1))
                transpose_columns(xres, bank[4:6], x1_tp)

            with pe.Fori(0, NOUT // 2 - 1) as m:
                n = m * 2 + 1
                for k in range(2):
                    pe.wait_ge(acc_free, n + (G_OUT + k - 1))
                    for i in range(HALVES):
                        half(n + (G_OUT + k), i, (1 + k) % 2)
                        if i == 4:
                            x1_transpose(n + (k - 1))
            pe.wait_ge(acc_free, G_GATE - 2)
            for i in range(HALVES):
                half(G_GATE - 1, i, 1)
                if i == 4:
                    x1_transpose(NOUT - 2)

            def project(n):
                pe.wait_ge(wp_in, n * 16 + 16)
                if not (isinstance(n, int) and n == 0):
                    pe.wait_ge(gated_proj, n)
                for t in range(TOK):
                    for j in range(PLE_T):
                        last = nc.tensor.matmul(bank[6 + t][:, :], pT[:, j, t * P:(t + 1) * P], wp[:, j, :],
                                                start=(j == 0), stop=(j == PLE_T - 1))
                last.then_inc(proj_ps, 1)

            pe.wait_ge(acc_free, G_GATE - 1)
            pe.wait_ge(p_T, 1)
            for i in range(HALVES):
                pe.wait_ge(conv_lo, HALVES + i + 1)
                half(G_GATE, i, 0)
                if i == 4:
                    x1_transpose(NOUT - 1)
                elif i == 12:
                    project(0)
            pe.wait_ge(acc_free, G_GATE)
            with pe.Fori(0, NOUT // 2 - 1) as m:
                n = m * 2 + 1
                for k in range(2):
                    pe.wait_ge(gate_read, n + (k - 1))
                    for i in range(HALVES):
                        half(n + (G_GATE + k), i, (1 + k) % 2)
                        if i == 12:
                            project(n + k)
            pe.wait_ge(gate_read, NOUT - 2)
            for i in range(HALVES):
                half(G_GATE + NOUT - 1, i, 1)
                if i == 12:
                    project(NOUT - 1)


_INS = ["x", "p", "norm_g", "attn_w_in", "attn_q_norm_g", "attn_k_norm_g", "attn_sink", "attn_w_out", "ple_norm_g",
        "ple_w_gate", "ple_w_proj"]


def kernel(**inputs):
    import numpy as _np
    import concourse.bacc as _bacc
    from concourse import mybir as _mybir
    from concourse.bass_utils import run_bass_kernel_spmd as _run

    nc = _bacc.Bacc("TRN2", target_bir_lowering=False, num_devices=1)
    arrays, args = {}, []
    for name in _INS:
        a = _np.ascontiguousarray(inputs[name])
        arrays[f"in_{name}_dram"] = a
        args.append(nc.dram_tensor(f"in_{name}_dram", a.shape, _mybir.dt.from_np(a.dtype), kind="ExternalInput").ap())
    result = nc.dram_tensor("out_dram", (1, SEQ, D_MODEL), _mybir.dt.float32, kind="ExternalOutput").ap()
    x, p, norm_g, w_in, q_g, k_g, sink, w_out, ple_g, w_gate, w_proj = args
    encoder_layer(nc, x, p, norm_g, w_in, q_g, k_g, sink, w_out, ple_g, w_gate, w_proj, result)
    r = _run(nc, [arrays], core_ids=[0])
    return r.results[0]["out_dram"]
```

```python
import concourse.bass as bass
from concourse import mybir
from contextlib import ExitStack

F32 = mybir.dt.float32
F32R = mybir.dt.float32r
I32 = mybir.dt.int32
ALU = mybir.AluOpType
ACT = mybir.ActivationFunctionType
X_AXIS = mybir.AxisListType.X

P = 128
SEQ = 256
D_MODEL = 4096
TOK = SEQ // P
KT = D_MODEL // P
N = 512
HEAD_DIM = 128
N_KV = 8
GROUP = 4
KV_W = N_KV * HEAD_DIM
Q_W = D_MODEL
PLE = 256
PLE_T = PLE // P
EPS = 1e-6
SCALE = HEAD_DIM ** -0.5
WINDOW = 128
MASKED = -1e36

HALVES = KT // 2
RING = 4
AHEAD = RING

G_K, G_V, G_Q0 = 0, 2, 4
G_Z = lambda c: 5 + 2 * c
G_OUT = G_Z(N_KV - 1) + 1
G_GATE = G_OUT + D_MODEL // N
G_PROJ = G_GATE + D_MODEL // N
NOUT = D_MODEL // N


def encoder_layer(nc, x, p, norm_g, w_in, q_g, k_g, sink, w_out, ple_g, w_gate, w_proj, out):
    x = x[0]
    p = p[0, 0]
    w_in, w_out, w_gate, w_proj, out = w_in[0], w_out[0], w_gate[0], w_proj[0], out[0]
    ctx = ExitStack()
    with ctx:
        def sb(name, shape, dt=F32):
            return ctx.enter_context(nc.sbuf_tensor(name, shape, dt))

        def sem(name):
            return ctx.enter_context(nc.semaphore(name))

        aT_hi = sb("aT_hi", [P, KT, SEQ], F32R)
        aT_lo = sb("aT_lo", [P, KT, SEQ], F32R)
        stage = sb("stage", [P, KT * SEQ])
        x_in = stage[:, :].rearrange("q (t n) -> q t n", t=TOK)
        gates = x_in
        nextT = stage[:, :].rearrange("q (j t) -> q j t", t=SEQ)
        raw = sb("raw", [P, RING, 2 * N])
        w_hi = sb("w_hi", [P, RING, 2 * N], F32R)
        w_lo = sb("w_lo", [P, RING, 2 * N], F32R)
        kc_hi, kc_lo = sb("kc_hi", [P, SEQ], F32R), sb("kc_lo", [P, SEQ], F32R)
        vc_hi, vc_lo = sb("vc_hi", [P, TOK, HEAD_DIM], F32R), sb("vc_lo", [P, TOK, HEAD_DIM], F32R)
        qT_hi, qT_lo = sb("qT_hi", [P, TOK, GROUP * P], F32R), sb("qT_lo", [P, TOK, GROUP * P], F32R)
        PT_hi, PT_lo = sb("PT_hi", [P, TOK, GROUP * P], F32R), sb("PT_lo", [P, TOK, GROUP * P], F32R)
        pT_hi = qT_hi[:, 0, :].rearrange("q (j t) -> q j t", j=PLE_T)
        pT_lo = qT_lo[:, 0, :].rearrange("q (j t) -> q j t", j=PLE_T)
        arena = sb("arena", [P, 10240])

        def at(a, size):
            return arena[:, a:a + size]

        kT = at(0, 2048).rearrange("q (h s) -> q h s", h=N_KV)
        v_sb = at(2048, 2048).rearrange("q (t n) -> q t n", t=TOK)
        bias = at(4096, 1536).rearrange("q (h s) -> q h s", h=GROUP)
        S = at(5632, 1024).rearrange("q (h s) -> q h s", h=GROUP)
        squares = at(5632, 1024)
        qk = at(6656, 1024).rearrange("q (t n) -> q t n", t=TOK)
        sg = qk
        oT = at(7680, 1024).rearrange("q (b n) -> q b n", b=TOK)
        vecs = at(8704, P)
        dist_i = at(8832, 384).bitcast(I32)
        dist = at(9216, 384)
        x1 = at(0, 8192).rearrange("q (t n) -> q t n", t=TOK)
        xres = at(8192, 1024).rearrange("q (t n) -> q t n", t=TOK)
        p_in = at(9216, TOK * PLE).rearrange("q (t n) -> q t n", t=TOK)
        junk = at(9216, 1024).rearrange("q (t n) -> q t n", t=TOK)
        o_out = [at(8192 + 1024 * k, 1024).rearrange("q (t n) -> q t n", t=TOK) for k in range(2)]

        ident = sb("ident", [P, P])
        NV = 2 * KT + 2
        vecT = sb("vecT", [P, NV])
        g1T, g2T, qgT, kgT = vecT[:, 0:KT], vecT[:, KT:2 * KT], vecT[:, 2 * KT:2 * KT + 1], vecT[:, 2 * KT + 1:NV]
        nsink = sb("nsink", [P, N_KV * GROUP])
        ss0 = sb("ss0", [P, TOK, 4])
        ss1 = sb("ss1", [P, TOK, NOUT])
        ssr = sb("ssr", [P, TOK])
        r = sb("r", [P, TOK])
        mhalf = sb("mhalf", [P, TOK * GROUP])
        half = sb("half", [P, GROUP])
        ssq = sb("ssq", [P, TOK * GROUP])
        rstd = sb("rstd", [P, TOK, GROUP])
        nm = sb("nm", [P, TOK, GROUP])
        sd = sb("sd", [P, TOK, GROUP])
        den = sb("den", [P, TOK, GROUP])
        rinv = sb("rinv", [P, TOK, GROUP])

        bank = [ctx.enter_context(nc.psum_tensor(f"bank{i}", [P, N], F32)) for i in range(8)]
        acc = [bank[0:2], bank[2:4]]

        raw_in = [sem(f"raw_in{i}") for i in range(RING)]
        hi_done, lo_done = sem("hi_done"), sem("lo_done")
        pe_half = sem("pe_half")
        acc_free = sem("acc_free")
        x_landed = [sem(f"x_landed{i}") for i in range(8)]
        vec_landed, sink_landed = sem("vec_landed"), sem("sink_landed")
        ident_zero, ident_ready = sem("ident_zero"), sem("ident_ready")
        iota_ready, dist_f, dist_neg = sem("iota_ready"), sem("dist_f"), sem("dist_neg")
        dist_mask, bias_ready = sem("dist_mask"), sem("bias_ready")
        exponent_ready = sem("exponent_ready")
        vec_tp, vec_ready, nsink_ready = sem("vec_tp"), sem("vec_ready"), sem("nsink_ready")
        xT_ps, xT_hi, xT_lo = sem("xT_ps"), sem("xT_hi"), sem("xT_lo")
        ss0_part, ss_sum, mean_ready, r_ready = sem("ss0_part"), sem("ss_sum"), sem("mean_ready"), sem("r_ready")
        qk_sb, qk_sq, qk_ss, qk_mean, qk_rstd = (sem("qk_sb"), sem("qk_sq"), sem("qk_ss"), sem("qk_mean"),
                                                 sem("qk_rstd"))
        k_normed, qk_tp, qk_T, qT_split = sem("k_normed"), sem("qk_tp"), sem("qk_T"), sem("qT_split")
        kv_hi, kv_lo = sem("kv_hi"), sem("kv_lo")
        scores_ps, scores_sb, rowmax, max_ready = (sem("scores_ps"), sem("scores_sb"), sem("rowmax"),
                                                   sem("max_ready"))
        sink_diff, exp_ready, probs_ready = sem("sink_diff"), sem("exp_ready"), sem("probs_ready")
        probs_tp, probs_hi, probs_lo = sem("probs_tp"), sem("probs_hi"), sem("probs_lo")
        den_sum, rinv_ready, o_ps, o_ready = sem("den_sum"), sem("rinv_ready"), sem("o_ps"), sem("o_ready")
        sg_ready, sz_tp, go_T = sem("sg_ready"), sem("sz_tp"), sem("go_T")
        conv_hi, conv_lo = sem("conv_hi"), sem("conv_lo")
        xres_in, x1_kept, x1_tp, x1_T, x1_sq = (sem("xres_in"), sem("x1_kept"), sem("x1_tp"), sem("x1_T"),
                                                sem("x1_sq"))
        p_landed, p_tp, pT_top, pT_split = sem("p_landed"), sem("p_tp"), sem("pT_top"), sem("pT_split")
        gated_proj, out_ready = sem("gated_proj"), sem("out_ready")
        out_stored = [sem(f"out_stored{k}") for k in range(2)]

        block = ctx.enter_context(nc.Block())

        @block.sync
        def _(sp):
            def load(h, i, w, col):
                if not (isinstance(h, int) and h < RING):
                    sp.wait_ge(lo_done, h - (RING - 1))
                src = w[2 * P * i:2 * P * (i + 1), bass.ds(col, N)].rearrange("(a q) n -> q a n", q=P)
                dst = raw[:, i % RING, :].rearrange("q (a n) -> q a n", a=2)
                sp.dma_start(dst, src).then_inc(raw_in[i % RING], 16)

            def chunk(g, w, col):
                for i in range(HALVES):
                    load(g * HALVES + i, i, w, col)

            def load_x(k):
                cols = slice(k * N, (k + 1) * N)
                sp.dma_start(x_in[:, :, cols], x[:, cols].rearrange("(t q) n -> q t n", q=P))\
                  .then_inc(x_landed[k], 16)

            x_after = {1: 1, 3: 2, 5: 4, 7: 5, 9: 6, 11: 7}
            load_x(0)
            for i in range(HALVES):
                load(i, i, w_in, Q_W)
                if i in x_after:
                    load_x(x_after[i])
                if i == 3:
                    load_x(3)
            with sp.Fori(1, G_Q0) as g:
                chunk(g, w_in, g * N + Q_W)
            chunk(G_Q0, w_in, 0)
            with sp.Fori(0, N_KV - 1) as c:
                chunk(c * 2 + G_Z(0), w_in, c * N + (Q_W + 2 * KV_W))
                chunk(c * 2 + (G_Z(0) + 1), w_in, c * N + N)
            chunk(G_Z(N_KV - 1), w_in, Q_W + 2 * KV_W + (N_KV - 1) * N)
            with sp.Fori(0, NOUT) as n:
                chunk(n + G_OUT, w_out, n * N)
            with sp.Fori(0, NOUT) as n:
                chunk(n + G_GATE, w_gate, n * N)
            for n in range(NOUT):
                sp.wait_ge(lo_done, G_PROJ * HALVES + n - (RING - 1))
                src = w_proj[:, n * N:(n + 1) * N].rearrange("(a q) n -> q a n", q=P)
                sp.dma_start(raw[:, n % RING, :].rearrange("q (a n) -> q a n", a=2), src)\
                  .then_inc(raw_in[n % RING], 16)

        @block.gpsimd
        def _(pool):
            pool.memset(ident[:, :], 0.0).then_inc(ident_zero, 1)
            pool.wait_ge(ident_zero, 1)
            pool.affine_select(out=ident[:, :], in_=ident[:, :], compare_op=ALU.not_equal, fill=1.0, base=0,
                               pattern=[[-1, P]], channel_multiplier=1).then_inc(ident_ready, 1)
            pool.memset(half[:, :], 0.5).then_inc(exponent_ready, 1)
            pool.memset(mhalf[:, :], -0.5).then_inc(exponent_ready, 1)
            pool.iota(dist_i, pattern=[[-1, 3 * P]], base=P, channel_multiplier=1).then_inc(iota_ready, 1)
            pool.wait_ge(dist_neg, 1)
            pool.affine_select(out=dist, in_=dist, compare_op=ALU.is_ge, fill=MASKED, base=P + WINDOW,
                               pattern=[[-1, 3 * P]], channel_multiplier=1).then_inc(dist_mask, 1)
            pool.wait_ge(dist_mask, 1)
            pool.affine_select(out=dist, in_=dist, compare_op=ALU.is_ge, fill=MASKED, base=WINDOW - P,
                               pattern=[[1, 3 * P]], channel_multiplier=-1).then_inc(dist_mask, 1)
            pool.wait_ge(dist_mask, 2)
            for h in range(GROUP):
                last = pool.tensor_scalar(bias[:, h, :], dist, 2.0 ** (-8.0 * (h + 1) / (N_KV * GROUP)), None,
                                          ALU.mult)
            last.then_inc(bias_ready, 1)
            pool.wait_ge(exponent_ready, 2)

            rstd_flat = rstd[:, :, :].rearrange("q t h -> q (t h)")
            pool.wait_ge(mean_ready, 1)
            pool.tensor_tensor(r[:, :], ssr[:, :], mhalf[:, 0:TOK], ALU.pow).then_inc(r_ready, 1)
            for e in range(2):
                pool.wait_ge(qk_mean, e + 1)
                pool.tensor_tensor(rstd_flat, ssq[:, :], mhalf[:, :], ALU.pow).then_inc(qk_rstd, 1)

            def group(c):
                pool.wait_ge(qk_mean, c + 3)
                pool.tensor_tensor(rstd_flat, ssq[:, :], mhalf[:, :], ALU.pow).then_inc(qk_rstd, 1)

            with pool.Fori(0, N_KV - 1) as c:
                group(c)
                pool.wait_ge(scores_sb, c * 2 + 2)
                pool.tensor_tensor(bias, bias, half[:, :].unsqueeze(2).to_broadcast([P, GROUP, 3 * P]), ALU.mult)\
                    .then_inc(bias_ready, 1)
            group(N_KV - 1)
            with pool.Fori(0, NOUT) as n:
                pool.wait_ge(acc_free, n + (G_OUT + 1))
                pool.tensor_copy(x1[:, :, bass.ds(n * N, N)], xres).then_inc(x1_kept, 1)
            pool.wait_ge(mean_ready, 2)
            pool.tensor_tensor(r[:, :], ssr[:, :], mhalf[:, 0:TOK], ALU.pow).then_inc(r_ready, 1)

        @block.scalar
        def _(act):
            def hi_half(g, i):
                act.wait_ge(raw_in[i % RING], g * (16 * HALVES // RING) + 16 * (i // RING + 1))
                if not (isinstance(g, int) and g == 0 and i < RING):
                    act.wait_ge(pe_half, g * HALVES + (i - RING + 1))
                nc.scalar.activation(w_hi[:, i % RING, :], raw[:, i % RING, :], ACT.Copy).then_inc(hi_done, 1)

            for row, src in ((0, norm_g), (KT, ple_g)):
                act.dma_start(vecs[row:row + KT, :], src[0, :].rearrange("(j q) -> j q", q=P)).then_inc(vec_landed, 16)
            for row, src in ((2 * KT, q_g), (2 * KT + 1, k_g)):
                act.dma_start(vecs[row:row + 1, :], src[0:1, :]).then_inc(vec_landed, 16)
            act.dma_start(nsink[:, :], sink[0, :].partition_broadcast(P)).then_inc(sink_landed, 16)

            def xT_hi_pair(i):
                act.wait_ge(xT_ps, i + 1)
                for jj in range(2):
                    j = 2 * i + jj
                    last = nc.scalar.activation(aT_hi[:, j, :], bank[4 + i % 4][:, jj * SEQ:(jj + 1) * SEQ],
                                                ACT.Copy, scale=g1T[:, j:j + 1])
                last.then_inc(xT_hi, 1)

            def k_transposed(e):
                act.wait_ge(qk_tp, e + 1)
                for t in range(TOK):
                    last = nc.scalar.activation(kT[:, 4 * e:4 * e + 4, t * P:(t + 1) * P],
                                                bank[4 + t][:, :].rearrange("q (h n) -> q h n", h=GROUP),
                                                ACT.Copy, scale=kgT)
                last.then_inc(qk_T, 1)

            def q_transposed(c):
                act.wait_ge(qk_tp, c + 3)
                for t in range(TOK):
                    last = nc.scalar.activation(qT_hi[:, t, :], bank[4 + t][:, :], ACT.Copy, scale=qgT)
                last.then_inc(qk_T, 1)

            def split_kv(c):
                nc.scalar.activation(kc_hi[:, :], kT[:, bass.ds(c, 1), :].rearrange("q a s -> q (a s)"), ACT.Copy)
                nc.scalar.activation(vc_hi[:, :, :], v_sb[:, :, bass.ds(c * HEAD_DIM, HEAD_DIM)], ACT.Copy)\
                  .then_inc(kv_hi, 1)

            def exps(c, b):
                act.wait_ge(max_ready, c * 2 + (b + 1))
                for h in range(GROUP):
                    nc.scalar.activation(S[:, h, :], S[:, h, :], ACT.Exp, bias=nm[:, b, h:h + 1],
                                         accum_out=den[:, b, h:h + 1])
                nc.scalar.activation(sd[:, b, :], sd[:, b, :], ACT.Exp).then_inc(exp_ready, 1)

            def probs_transposed(c, b):
                act.wait_ge(probs_tp, c * 2 + (b + 1))
                for s in range(TOK):
                    last = nc.scalar.activation(PT_hi[:, s, :], bank[4 + s][:, :], ACT.Copy)
                last.then_inc(probs_hi, 1)

            def outputs_transposed(c, b):
                act.wait_ge(o_ps, c * 2 + (b + 1))
                nc.scalar.activation(oT[:, b, :], bank[4][:, :], ACT.Copy).then_inc(o_ready, 1)

            def z_sigmoid(c):
                act.wait_ge(pe_half, (c * 2 + (G_Z(0) + 1)) * HALVES)
                for t in range(TOK):
                    last = nc.scalar.activation(sg[:, t, :], acc[1][t][:, :], ACT.Sigmoid, scale=r[:, t:t + 1])
                last.then_inc(sg_ready, 1)

            def convert_hi(phase, i, g_before, written, count):
                act.wait_ge(pe_half, g_before * HALVES + i + 1)
                act.wait_ge(written, count)
                nc.scalar.activation(aT_hi[:, 2 * i:2 * i + 2, :], nextT[:, 2 * i:2 * i + 2, :], ACT.Copy)\
                  .then_inc(conv_hi, 1)

            def x1_transposed(n):
                act.wait_ge(x1_tp, n + 1)
                for jj in range(4):
                    b = bank[4 + jj // 2][:, (jj % 2) * SEQ:(jj % 2 + 1) * SEQ]
                    last = nc.scalar.activation(nextT[:, bass.ds(n * 4 + jj, 1), :].rearrange("q a t -> q (a t)"), b,
                                                ACT.Copy, scale=g2T[:, bass.ds(n * 4 + jj, 1)])
                last.then_inc(x1_T, 1)

            def x1_squares(n):
                act.wait_ge(acc_free, n + (G_OUT + 1))
                for t in range(TOK):
                    last = nc.scalar.activation(junk[:, t, :], xres[:, t, :], ACT.Square,
                                                accum_out=ss1[:, t, bass.ds(n, 1)])
                last.then_inc(x1_sq, 1)

            def load_residual(n):
                if not (isinstance(n, int) and n == 0):
                    act.wait_ge(x1_sq, n)
                    act.wait_ge(x1_kept, n)
                act.dma_start(xres, x[:, bass.ds(n * N, N)].rearrange("(t q) n -> q t n", q=P)).then_inc(xres_in, 16)

            def gate_sigmoid(n, pair):
                act.wait_ge(pe_half, (n + (G_GATE + 1)) * HALVES)
                for t in range(TOK):
                    last = nc.scalar.activation(gates[:, t, bass.ds(n * N, N)], acc[pair][t][:, :], ACT.Sigmoid,
                                                scale=r[:, t:t + 1])
                last.then_inc(acc_free, 1)

            act.wait_ge(vec_tp, 1)
            nc.scalar.activation(vecT[:, :], bank[7][:, 0:NV], ACT.Copy).then_inc(vec_ready, 1)
            act.wait_ge(vec_ready, 1)
            for i in range(HALVES):
                xT_hi_pair(i)
                hi_half(0, i)
            for g in (1, 2, 3, 4):
                for i in range(HALVES):
                    hi_half(g, i)
                    if i == 7 and g <= 2:
                        k_transposed(g - 1)
                    elif i == 7 and g == 4:
                        act.wait_ge(qk_T, 2)
                        act.wait_ge(acc_free, 4)
                        split_kv(0)

            def attention(c, i):
                if i == 5:
                    q_transposed(c)
                elif i == 8:
                    exps(c, 0)
                elif i == 10:
                    probs_transposed(c, 0)
                elif i == 13:
                    exps(c, 1)
                    outputs_transposed(c, 0)
                elif i == 15:
                    probs_transposed(c, 1)

            def gating(c, i):
                if i == 1:
                    outputs_transposed(c, 1)
                elif i == 2:
                    z_sigmoid(c)

            with act.Fori(0, N_KV - 1) as c:
                for i in range(HALVES):
                    hi_half(c * 2 + G_Z(0), i)
                    attention(c, i)
                for i in range(HALVES):
                    hi_half(c * 2 + (G_Z(0) + 1), i)
                    gating(c, i)
                    if i == 9:
                        split_kv(c + 1)

            c = N_KV - 1
            for i in range(HALVES):
                hi_half(G_Z(c), i)
                attention(c, i)
                if i >= AHEAD:
                    convert_hi(0, i - AHEAD, G_Z(c), go_T, (i - AHEAD) // 2 + 1)
            for i in range(HALVES):
                hi_half(G_OUT, i)
                if i == 0:
                    act.dma_start(p_in, p.rearrange("(t q) n -> q t n", q=P)).then_inc(p_landed, 16)
                gating(c, i)
                if i < 2:
                    convert_hi(0, 12 + i, G_Z(c), go_T, (12 + i) // 2 + 1)
                elif i in (8, 9):
                    convert_hi(0, 6 + i, G_Z(c), go_T, N_KV)
                elif i == 10:
                    act.wait_ge(go_T, N_KV)
                    load_residual(0)
                elif i == 11:
                    act.wait_ge(p_tp, 1)
                    nc.scalar.activation(qT_hi[:, 0, :], bank[6][:, :], ACT.Copy).then_inc(pT_top, 1)

            def out_chunk(n):
                for i in range(HALVES):
                    hi_half(n + G_OUT, i)
                    if i == 7:
                        x1_transposed(n - 1)
                    elif i == 9:
                        x1_squares(n - 1)
                    elif i == 10:
                        load_residual(n)

            act.wait_ge(conv_lo, HALVES)
            with act.Fori(1, NOUT - 1) as n:
                out_chunk(n)
            n = NOUT - 1
            for i in range(HALVES):
                hi_half(n + G_OUT, i)
                if i == 7:
                    x1_transposed(n - 1)
                elif i == 9:
                    x1_squares(n - 1)
                elif i == 10:
                    load_residual(n)
                if i >= AHEAD:
                    convert_hi(1, i - AHEAD, G_GATE - 1, x1_T, (i - AHEAD) // 2 + 1)
            for i in range(HALVES):
                hi_half(G_GATE, i)
                if i < 2:
                    convert_hi(1, 12 + i, G_GATE - 1, x1_T, (12 + i) // 2 + 1)
                elif i == 7:
                    x1_transposed(NOUT - 1)
                elif i in (8, 9):
                    convert_hi(1, 6 + i, G_GATE - 1, x1_T, NOUT)
                elif i == 10:
                    x1_squares(NOUT - 1)

            def gate_chunk(n, pair):
                for i in range(HALVES):
                    hi_half(n + G_GATE, i)
                    if i == 2:
                        gate_sigmoid(n - 1, pair)

            act.wait_ge(r_ready, 2)
            with act.Fori(0, NOUT // 2 - 1) as m:
                n = m * 2 + 1
                gate_chunk(n, 0)
                gate_chunk(n + 1, 1)
            gate_chunk(NOUT - 1, 0)

            def store(n):
                for t in range(TOK):
                    act.wait_ge(out_ready, TOK * n + t + 1)
                    act.dma_start(out[t * P:(t + 1) * P, n * N:(n + 1) * N], o_out[n % 2][:, t, :])\
                       .then_inc(out_stored[n % 2], 16)

            for n in range(NOUT):
                hi_half(G_PROJ, n)
                if n == 2:
                    gate_sigmoid(NOUT - 1, 1)
                if n >= AHEAD:
                    store(n - AHEAD)
            for n in range(NOUT - AHEAD, NOUT):
                store(n)
            for k in range(2):
                act.wait_ge(out_stored[k], 16 * NOUT)

        @block.vector
        def _(dve):
            def lo_half(g, i):
                dve.wait_ge(hi_done, g * HALVES + (i + 1))
                nc.vector.tensor_tensor(w_lo[:, i % RING, :], raw[:, i % RING, :],
                                        w_hi[:, i % RING, :].bitcast(F32), ALU.subtract).then_inc(lo_done, 1)

            dve.wait_ge(iota_ready, 1)
            nc.vector.tensor_copy(dist, dist_i).then_inc(dist_f, 1)
            dve.wait_ge(dist_f, 1)
            nc.vector.scalar_tensor_tensor(dist, dist, -1.0, dist, ALU.mult, ALU.min).then_inc(dist_neg, 1)
            dve.wait_ge(sink_landed, 16)
            nc.vector.tensor_scalar(nsink[:, :], nsink[:, :], -1.0, None, ALU.mult).then_inc(nsink_ready, 1)
            dve.wait_ge(vec_ready, 1)

            for i in range(HALVES):
                dve.wait_ge(xT_hi, i + 1)
                for jj in range(2):
                    j = 2 * i + jj
                    last = nc.vector.scalar_tensor_tensor(aT_lo[:, j, :], bank[4 + i % 4][:, jj * SEQ:(jj + 1) * SEQ],
                                                          g1T[:, j:j + 1], aT_hi[:, j, :].bitcast(F32), ALU.mult,
                                                          ALU.subtract)
                last.then_inc(xT_lo, 1)
                lo_half(0, i)
                if i % 2 == 1:
                    t, k = (i // 2) % 2, i // 4
                    dve.wait_ge(x_landed[2 * k], 16)
                    dve.wait_ge(x_landed[2 * k + 1], 16)
                    if i > 1:
                        dve.wait_ge(ss0_part, i // 2)
                    xs = x_in[:, t, k * 1024:(k + 1) * 1024]
                    nc.vector.scalar_tensor_tensor(squares, xs, 1.0, xs, ALU.mult, ALU.mult,
                                                   accum_out=ss0[:, t, k:k + 1]).then_inc(ss0_part, 1)
            dve.wait_ge(ss0_part, 8)
            nc.vector.tensor_reduce(ssr[:, :], ss0[:, :, :], X_AXIS, ALU.add).then_inc(ss_sum, 1)
            dve.wait_ge(ss_sum, 1)
            nc.vector.tensor_scalar(ssr[:, :], ssr[:, :], 1.0 / D_MODEL, EPS, ALU.mult, ALU.add)\
              .then_inc(mean_ready, 1)

            def evacuate(g, pair, dsts):
                dve.wait_ge(pe_half, g * HALVES + HALVES)
                for t in range(TOK):
                    last = nc.vector.tensor_scalar(dsts[t], acc[pair][t][:, :], r[:, t:t + 1], None, ALU.mult)
                last.then_inc(acc_free, 1)

            def qk_squares(g):
                dve.wait_ge(acc_free, g + 1)
                flat = qk.rearrange("q t n -> q (t n)")
                nc.vector.tensor_tensor(squares, flat, flat, ALU.mult).then_inc(qk_sq, 1)

            def qk_sums(e, scale=1.0):
                dve.wait_ge(qk_sq, e + 1)
                nc.vector.tensor_reduce(ssq[:, :], squares.rearrange("q (h n) -> q h n", n=HEAD_DIM), X_AXIS,
                                        ALU.add).then_inc(qk_ss, 1)
                dve.wait_ge(qk_ss, e + 1)
                nc.vector.tensor_scalar(ssq[:, :], ssq[:, :], 1.0 / (HEAD_DIM * scale ** 2), EPS / scale ** 2, ALU.mult,
                                        ALU.add)\
                  .then_inc(qk_mean, 1)

            def split_kv(c):
                dve.wait_ge(kv_hi, c + 1)
                nc.vector.tensor_tensor(kc_lo[:, :], kT[:, bass.ds(c, 1), :].rearrange("q a s -> q (a s)"),
                                        kc_hi[:, :].bitcast(F32), ALU.subtract)
                nc.vector.tensor_tensor(vc_lo[:, :, :], v_sb[:, :, bass.ds(c * HEAD_DIM, HEAD_DIM)],
                                        vc_hi[:, :, :].bitcast(F32), ALU.subtract).then_inc(kv_lo, 1)

            dve.wait_ge(r_ready, 1)
            for g in (1, 2, 3, 4):
                for i in range(HALVES):
                    lo_half(g, i)
                    e = g - 1
                    if i == 2 and g <= 2:
                        evacuate(e, e % 2, [qk[:, t, :] for t in range(TOK)])
                    elif i == 2:
                        evacuate(e, e % 2, [v_sb[:, t, (e - 2) * N:(e - 1) * N] for t in range(TOK)])
                    elif i == 3 and g <= 2:
                        qk_squares(e)
                        qk_sums(e)
                    elif i == 5 and g <= 2:
                        dve.wait_ge(qk_rstd, e + 1)
                        nc.vector.tensor_tensor(
                            qk.rearrange("q t (h n) -> q (t h) n", n=HEAD_DIM),
                            qk.rearrange("q t (h n) -> q (t h) n", n=HEAD_DIM),
                            rstd[:, :, :].rearrange("q t h -> q (t h)").unsqueeze(2)
                                .to_broadcast([P, TOK * GROUP, HEAD_DIM]), ALU.mult).then_inc(k_normed, 1)
                    elif i == 8 and g == 4:
                        split_kv(0)

            def q_lo(c):
                dve.wait_ge(qk_T, c + 3)
                for t in range(TOK):
                    last = nc.vector.scalar_tensor_tensor(qT_lo[:, t, :], bank[4 + t][:, :], qgT,
                                                          qT_hi[:, t, :].bitcast(F32), ALU.mult, ALU.subtract)
                last.then_inc(qT_split, 1)

            def score_rows(c, b):
                dve.wait_ge(scores_ps, c * 2 + (b + 1))
                if b == 0:
                    dve.wait_ge(bias_ready, c + 1)
                    dve.wait_ge(qk_rstd, c + 3)
                else:
                    dve.wait_ge(probs_tp, c * 2 + 1)
                for h in range(GROUP):
                    ps = bank[6 + h // 2][:, (h % 2) * SEQ:(h % 2 + 1) * SEQ]
                    last = nc.vector.scalar_tensor_tensor(S[:, h, :], ps, rstd[:, b, h:h + 1],
                                                          bias[:, h, P * (1 - b):P * (1 - b) + SEQ], ALU.mult, ALU.add)
                last.then_inc(scores_sb, 1)

            def maxima(c, b):
                k = c * 2 + (b + 1)
                dve.wait_ge(scores_sb, k)
                nc.vector.tensor_reduce(nm[:, b, :], S, X_AXIS, ALU.max, negate=True).then_inc(rowmax, 1)
                dve.wait_ge(rowmax, k)
                sinks = nsink[:, bass.ds(c * GROUP, GROUP)]
                nc.vector.tensor_tensor(nm[:, b, :], nm[:, b, :], sinks, ALU.min).then_inc(sink_diff, 1)
                dve.wait_ge(sink_diff, k)
                nc.vector.tensor_tensor(sd[:, b, :], nm[:, b, :], sinks, ALU.subtract).then_inc(max_ready, 1)

            def normalize(c, b):
                k = c * 2 + (b + 1)
                dve.wait_ge(exp_ready, k)
                nc.vector.tensor_tensor(den[:, b, :], den[:, b, :], sd[:, b, :], ALU.add).then_inc(den_sum, 1)
                dve.wait_ge(den_sum, k)
                nc.vector.reciprocal(rinv[:, b, :], den[:, b, :]).then_inc(rinv_ready, 1)
                dve.wait_ge(rinv_ready, k)
                nc.vector.tensor_tensor(S, S, rinv[:, b, :].unsqueeze(2).to_broadcast([P, GROUP, SEQ]), ALU.mult)\
                  .then_inc(probs_ready, 1)

            def probs_lo_part(c, b):
                dve.wait_ge(probs_hi, c * 2 + (b + 1))
                for s in range(TOK):
                    last = nc.vector.tensor_tensor(PT_lo[:, s, :], bank[4 + s][:, :], PT_hi[:, s, :].bitcast(F32),
                                                   ALU.subtract)
                last.then_inc(probs_lo, 1)

            def attention(c, i):
                g = c * 2 + G_Z(0)
                if i == 2:
                    evacuate(g - 1, 0, [qk[:, t, :] for t in range(TOK)])
                elif i == 3:
                    qk_squares(g - 1)
                elif i == 4:
                    qk_sums(c + 2, SCALE)
                elif i == 5:
                    q_lo(c)
                elif i == 6:
                    score_rows(c, 0)
                elif i == 7:
                    maxima(c, 0)
                elif i == 9:
                    normalize(c, 0)
                elif i == 10:
                    score_rows(c, 1)
                elif i == 11:
                    probs_lo_part(c, 0)
                elif i == 12:
                    maxima(c, 1)
                elif i == 14:
                    normalize(c, 1)

            def gating(c, i):
                if i == 0:
                    probs_lo_part(c, 1)
                elif i == 3:
                    dve.wait_ge(sg_ready, c + 1)
                    for t in range(TOK):
                        last = nc.vector.scalar_tensor_tensor(sg[:, t, :], acc[1][t][:, :], r[:, t:t + 1], sg[:, t, :],
                                                              ALU.mult, ALU.mult)
                    last.then_inc(acc_free, 1)
                elif i == 6:
                    dve.wait_ge(sz_tp, c + 1)
                    dve.wait_ge(o_ready, c * 2 + 2)
                    for jj in range(2):
                        heads = oT.rearrange("q b (h n) -> q h b n", h=GROUP)[:, 2 * jj:2 * jj + 2]
                        last = nc.vector.tensor_tensor(
                            nextT[:, bass.ds(c * 4 + 2 * jj, 2), :].rearrange("q h (b n) -> q h b n", b=TOK),
                            bank[4 + jj][:, :].rearrange("q (h b n) -> q h b n", h=2, b=TOK), heads, ALU.mult)
                    last.then_inc(go_T, 1)

            def convert_lo(k, i):
                dve.wait_ge(conv_hi, k)
                nc.vector.tensor_tensor(aT_lo[:, 2 * i:2 * i + 2, :], nextT[:, 2 * i:2 * i + 2, :],
                                        aT_hi[:, 2 * i:2 * i + 2, :].bitcast(F32), ALU.subtract).then_inc(conv_lo, 1)

            with dve.Fori(0, N_KV - 1) as c:
                for i in range(HALVES):
                    lo_half(c * 2 + G_Z(0), i)
                    attention(c, i)
                for i in range(HALVES):
                    lo_half(c * 2 + (G_Z(0) + 1), i)
                    gating(c, i)
                    if i == 10:
                        split_kv(c + 1)
            c = N_KV - 1
            for i in range(HALVES):
                lo_half(G_Z(c), i)
                attention(c, i)
                if i >= AHEAD:
                    convert_lo(i - AHEAD + 1, i - AHEAD)
            for i in range(HALVES):
                lo_half(G_OUT, i)
                gating(c, i)
                if i < 2:
                    convert_lo(13 + i, 12 + i)
                elif i in (8, 9):
                    convert_lo(7 + i, 6 + i)
                elif i == 12:
                    dve.wait_ge(pT_top, 1)
                    nc.vector.tensor_tensor(qT_lo[:, 0, :], bank[6][:, :], qT_hi[:, 0, :].bitcast(F32), ALU.subtract)\
                      .then_inc(pT_split, 1)

            def residual(n, pair):
                dve.wait_ge(pe_half, (n + (G_OUT + 1)) * HALVES)
                dve.wait_ge(xres_in, n * 16 + 16)
                for t in range(TOK):
                    last = nc.vector.tensor_tensor(xres[:, t, :], acc[pair][t][:, :], xres[:, t, :], ALU.add)
                last.then_inc(acc_free, 1)

            with dve.Fori(0, NOUT // 2 - 1) as m:
                n = m * 2 + 1
                for k in range(2):
                    for i in range(HALVES):
                        lo_half(n + (G_OUT + k), i)
                        if i == 2:
                            residual(n + (k - 1), k)
            for i in range(HALVES):
                lo_half(G_OUT + NOUT - 1, i)
                if i == 2:
                    residual(NOUT - 2, 0)
                if i >= AHEAD:
                    convert_lo(HALVES + i - AHEAD + 1, i - AHEAD)
            for i in range(HALVES):
                lo_half(G_GATE, i)
                if i < 2:
                    convert_lo(HALVES + 13 + i, 12 + i)
                if i == 2:
                    residual(NOUT - 1, 1)
                elif i == 12:
                    dve.wait_ge(x1_sq, NOUT)
                    nc.vector.tensor_reduce(ssr[:, :], ss1[:, :, :], X_AXIS, ALU.add).then_inc(ss_sum, 1)
                    dve.wait_ge(ss_sum, 2)
                    nc.vector.tensor_scalar(ssr[:, :], ssr[:, :], 1.0 / D_MODEL, EPS, ALU.mult, ALU.add)\
                      .then_inc(mean_ready, 1)
                if i in (8, 9):
                    convert_lo(HALVES + 7 + i, 6 + i)

            with dve.Fori(1, NOUT) as n:
                for i in range(HALVES):
                    lo_half(n + G_GATE, i)

            def output(n):
                cols = slice(n * N, (n + 1) * N)
                dve.wait_ge(pe_half, G_PROJ * HALVES + n + 1)
                if n == NOUT - 1:
                    dve.wait_ge(acc_free, G_PROJ)
                if n >= 2:
                    dve.wait_ge(out_stored[n % 2], 16 * TOK * (n // 2))
                for t in range(TOK):
                    nc.vector.tensor_tensor(o_out[n % 2][:, t, :], acc[n % 2][t][:, :], gates[:, t, cols], ALU.mult)\
                      .then_inc(gated_proj, 1)
                for t in range(TOK):
                    dve.wait_ge(gated_proj, TOK * n + t + 1)
                    nc.vector.tensor_tensor(o_out[n % 2][:, t, :], o_out[n % 2][:, t, :], x1[:, t, cols], ALU.add)\
                      .then_inc(out_ready, 1)

            dve.wait_ge(x1_kept, NOUT)
            dve.wait_ge(acc_free, G_PROJ - 1)
            for n in range(NOUT):
                lo_half(G_PROJ, n)
                if n >= AHEAD - 1:
                    output(n - (AHEAD - 1))
            for n in range(NOUT - (AHEAD - 1), NOUT):
                output(n)

        @block.tensor
        def _(pe):
            def products(outs, hi_of, lo_of, i, first, final):
                for jj in range(2):
                    whi = w_hi[:, i % RING, jj * N:(jj + 1) * N]
                    wlo = w_lo[:, i % RING, jj * N:(jj + 1) * N]
                    for t in range(TOK):
                        ahi, alo = hi_of(jj, t), lo_of(jj, t)
                        nc.tensor.matmul(outs[t][:, :], ahi, wlo, start=first and jj == 0, stop=False)
                        nc.tensor.matmul(outs[t][:, :], ahi, whi, start=False, stop=False)
                        last = nc.tensor.matmul(outs[t][:, :], alo, whi, start=False, stop=final and jj == 1)
                last.then_inc(pe_half, 1)

            def half(g, i, pair):
                pe.wait_ge(lo_done, g * HALVES + (i + 1))
                products(acc[pair], lambda jj, t: aT_hi[:, 2 * i + jj, t * P:(t + 1) * P],
                         lambda jj, t: aT_lo[:, 2 * i + jj, t * P:(t + 1) * P], i, i == 0, i == HALVES - 1)

            def transpose_tokens(src, banks, done):
                for t in range(TOK):
                    for h in range(GROUP):
                        last = nc.tensor.transpose(banks[t][:, h * P:(h + 1) * P], src[:, t, h * P:(h + 1) * P],
                                                   ident[:, :])
                last.then_inc(done, 1)

            def transpose_columns(src, banks, done):
                for j in range(4):
                    for t in range(TOK):
                        last = nc.tensor.transpose(banks[j // 2][:, (j % 2) * SEQ + t * P:(j % 2) * SEQ + (t + 1) * P],
                                                   src[:, t, j * P:(j + 1) * P], ident[:, :])
                last.then_inc(done, 1)

            def x_pair(i):
                if i % 2 == 0:
                    pe.wait_ge(x_landed[i // 2], 16)
                if i == 3:
                    pe.wait_ge(vec_ready, 1)
                if i >= 4:
                    pe.wait_ge(xT_lo, i - 3)
                for jj in range(2):
                    j = 2 * i + jj
                    for t in range(TOK):
                        last = nc.tensor.transpose(bank[4 + i % 4][:, jj * SEQ + t * P:jj * SEQ + (t + 1) * P],
                                                   x_in[:, t, j * P:(j + 1) * P], ident[:, :])
                last.then_inc(xT_ps, 1)

            pe.wait_ge(ident_ready, 1)
            pe.wait_ge(vec_landed, 64)
            nc.tensor.transpose(bank[7][:, 0:NV], vecs[0:NV, :], ident[0:NV, 0:NV]).then_inc(vec_tp, 1)
            for i in range(4):
                x_pair(i)
            for i in range(HALVES):
                pe.wait_ge(xT_lo, i + 1)
                half(0, i, 0)
                if i + 4 < HALVES:
                    x_pair(i + 4)

            for g in (1, 2, 3, 4):
                if g >= 2:
                    pe.wait_ge(acc_free, g - 1)
                for i in range(HALVES):
                    half(g, i, g % 2)
                    if i == 4 and g <= 2:
                        pe.wait_ge(k_normed, g)
                        if g == 2:
                            pe.wait_ge(qk_T, 1)
                        transpose_tokens(qk, bank[4:6], qk_tp)

            def scores(c, b):
                if b == 0:
                    pe.wait_ge(kv_lo, c + 1)
                    pe.wait_ge(qT_split, c + 1)
                else:
                    pe.wait_ge(scores_sb, c * 2 + 1)
                for h in range(GROUP):
                    ps = bank[6 + h // 2][:, (h % 2) * SEQ:(h % 2 + 1) * SEQ]
                    qhi, qlo = qT_hi[:, b, h * P:(h + 1) * P], qT_lo[:, b, h * P:(h + 1) * P]
                    nc.tensor.matmul(ps, qhi, kc_lo[:, :], start=True, stop=False)
                    nc.tensor.matmul(ps, qhi, kc_hi[:, :], start=False, stop=False)
                    last = nc.tensor.matmul(ps, qlo, kc_hi[:, :], start=False, stop=True)
                last.then_inc(scores_ps, 1)

            def transpose_probs(c, b):
                pe.wait_ge(probs_ready, c * 2 + (b + 1))
                if b == 1:
                    pe.wait_ge(o_ready, c * 2 + 1)
                for s in range(TOK):
                    for h in range(GROUP):
                        last = nc.tensor.transpose(bank[4 + s][:, h * P:(h + 1) * P], S[:, h, s * P:(s + 1) * P],
                                                   ident[:, :])
                last.then_inc(probs_tp, 1)

            def head_values(c, b):
                pe.wait_ge(probs_lo, c * 2 + (b + 1))
                for s in range(TOK):
                    nc.tensor.matmul(bank[4][:, :], vc_hi[:, s, :], PT_lo[:, s, :], start=(s == 0), stop=False)
                    nc.tensor.matmul(bank[4][:, :], vc_hi[:, s, :], PT_hi[:, s, :], start=False, stop=False)
                    last = nc.tensor.matmul(bank[4][:, :], vc_lo[:, s, :], PT_hi[:, s, :], start=False,
                                            stop=(s == TOK - 1))
                last.then_inc(o_ps, 1)

            def attention(c, i):
                if i == 1:
                    pe.wait_ge(acc_free, c * 2 + G_Z(0))
                    transpose_tokens(qk, bank[4:6], qk_tp)
                elif i == 3:
                    scores(c, 0)
                elif i == 5:
                    scores(c, 1)
                elif i == 7:
                    transpose_probs(c, 0)
                elif i == 10:
                    head_values(c, 0)
                elif i == 12:
                    transpose_probs(c, 1)
                elif i == 14:
                    head_values(c, 1)

            def gating(c, i):
                if i == 3:
                    pe.wait_ge(acc_free, c * 2 + (G_Z(0) + 1))
                    pe.wait_ge(o_ready, c * 2 + 2)
                    transpose_columns(sg, bank[4:6], sz_tp)

            with pe.Fori(0, N_KV - 1) as c:
                g = c * 2 + G_Z(0)
                pe.wait_ge(acc_free, g - 1)
                for i in range(HALVES):
                    half(g, i, 1)
                    attention(c, i)
                pe.wait_ge(acc_free, g)
                for i in range(HALVES):
                    half(g + 1, i, 0)
                    gating(c, i)
            c = N_KV - 1
            pe.wait_ge(acc_free, G_Z(c) - 1)
            for i in range(HALVES):
                half(G_Z(c), i, 1)
                attention(c, i)
            pe.wait_ge(acc_free, G_OUT - 1)
            for i in range(HALVES):
                pe.wait_ge(conv_lo, i + 1)
                half(G_OUT, i, 0)
                gating(c, i)
                if i == 8:
                    pe.wait_ge(p_landed, 16)
                    for j in range(PLE_T):
                        for t in range(TOK):
                            last = nc.tensor.transpose(bank[6][:, j * SEQ + t * P:j * SEQ + (t + 1) * P],
                                                       p_in[:, t, j * P:(j + 1) * P], ident[:, :])
                    last.then_inc(p_tp, 1)

            def x1_transpose(n):
                pe.wait_ge(acc_free, n + (G_OUT + 1))
                transpose_columns(xres, bank[4:6], x1_tp)

            with pe.Fori(0, NOUT // 2 - 1) as m:
                n = m * 2 + 1
                for k in range(2):
                    pe.wait_ge(acc_free, n + (G_OUT + k - 1))
                    for i in range(HALVES):
                        half(n + (G_OUT + k), i, (1 + k) % 2)
                        if i == 4:
                            x1_transpose(n + (k - 1))
            pe.wait_ge(acc_free, G_GATE - 2)
            for i in range(HALVES):
                half(G_GATE - 1, i, 1)
                if i == 4:
                    x1_transpose(NOUT - 2)

            pe.wait_ge(acc_free, G_GATE - 1)
            for i in range(HALVES):
                pe.wait_ge(conv_lo, HALVES + i + 1)
                half(G_GATE, i, 0)
                if i == 4:
                    x1_transpose(NOUT - 1)
            with pe.Fori(0, NOUT // 2 - 1) as m:
                n = m * 2 + 1
                for k in range(2):
                    pe.wait_ge(acc_free, n + (G_GATE + k - 1))
                    for i in range(HALVES):
                        half(n + (G_GATE + k), i, (1 + k) % 2)
            pe.wait_ge(acc_free, G_PROJ - 2)
            for i in range(HALVES):
                half(G_PROJ - 1, i, 1)

            pe.wait_ge(pT_split, 1)
            for n in range(NOUT):
                pe.wait_ge(lo_done, G_PROJ * HALVES + n + 1)
                if n < 2:
                    pe.wait_ge(acc_free, G_PROJ - 1 + n)
                else:
                    pe.wait_ge(gated_proj, TOK * (n - 1))
                products(acc[n % 2], lambda jj, t: pT_hi[:, jj, t * P:(t + 1) * P],
                         lambda jj, t: pT_lo[:, jj, t * P:(t + 1) * P], n, True, True)


_INS = ["x", "p", "norm_g", "attn_w_in", "attn_q_norm_g", "attn_k_norm_g", "attn_sink", "attn_w_out", "ple_norm_g",
        "ple_w_gate", "ple_w_proj"]


def kernel(**inputs):
    import numpy as _np
    import concourse.bacc as _bacc
    from concourse import mybir as _mybir
    from concourse.bass_utils import run_bass_kernel_spmd as _run

    nc = _bacc.Bacc("TRN2", target_bir_lowering=False, num_devices=1)
    arrays, args = {}, []
    for name in _INS:
        a = _np.ascontiguousarray(inputs[name])
        arrays[f"in_{name}_dram"] = a
        args.append(nc.dram_tensor(f"in_{name}_dram", a.shape, _mybir.dt.from_np(a.dtype), kind="ExternalInput").ap())
    result = nc.dram_tensor("out_dram", (1, SEQ, D_MODEL), _mybir.dt.float32, kind="ExternalOutput").ap()
    x, p, norm_g, w_in, q_g, k_g, sink, w_out, ple_g, w_gate, w_proj = args
    encoder_layer(nc, x, p, norm_g, w_in, q_g, k_g, sink, w_out, ple_g, w_gate, w_proj, result)
    r = _run(nc, [arrays], core_ids=[0])
    return r.results[0]["out_dram"]
```

```python
import concourse.bass as bass
from concourse import mybir
from contextlib import ExitStack

F32 = mybir.dt.float32
F32R = mybir.dt.float32r
I32 = mybir.dt.int32
ALU = mybir.AluOpType
ACT = mybir.ActivationFunctionType
X_AXIS = mybir.AxisListType.X

P = 128
SEQ = 256
D_MODEL = 4096
TOK = SEQ // P
KT = D_MODEL // P
N = 512
HEAD_DIM = 128
N_KV = 8
GROUP = 4
KV_W = N_KV * HEAD_DIM
Q_W = D_MODEL
PLE = 256
PLE_T = PLE // P
EPS = 1e-6
SCALE = HEAD_DIM ** -0.5
WINDOW = 128
MASKED = -1e36

HALVES = KT // 2
RING = 4
AHEAD = RING

G_Q0 = 4
G_Z = lambda c: 5 + 2 * c
G_OUT = G_Z(N_KV - 1) + 1
G_GATE = G_OUT + D_MODEL // N
G_PROJ = G_GATE + D_MODEL // N
NOUT = D_MODEL // N
POOL_SUMS = NOUT - 1
SQUARE_STEPS = (6, 8, 9, 11, 12, 14, 15)


def encoder_layer(nc, x, xT, pT, norm_gT, w_in, q_gT, k_gT, sink, w_out, ple_gT, w_gate, w_proj, out):
    x = x[0]
    w_in, w_out, w_gate, w_proj, out = w_in[0], w_out[0], w_gate[0], w_proj[0], out[0]
    ctx = ExitStack()
    with ctx:
        def sb(name, shape, dt=F32):
            return ctx.enter_context(nc.sbuf_tensor(name, shape, dt))

        def sem(name):
            return ctx.enter_context(nc.semaphore(name))

        aT_hi = sb("aT_hi", [P, KT, SEQ], F32R)
        aT_lo = sb("aT_lo", [P, KT, SEQ], F32R)
        stage = sb("stage", [P, KT * SEQ])
        gates = stage[:, :].rearrange("q (t n) -> q t n", t=TOK)
        nextT = stage[:, :].rearrange("q (j t) -> q j t", t=SEQ)
        raw = sb("raw", [P, RING, 2 * N])
        w_hi = sb("w_hi", [P, RING, 2 * N], F32R)
        w_lo = sb("w_lo", [P, RING, 2 * N], F32R)
        kc_hi, kc_lo = sb("kc_hi", [P, SEQ], F32R), sb("kc_lo", [P, SEQ], F32R)
        vc_hi, vc_lo = sb("vc_hi", [P, TOK, HEAD_DIM], F32R), sb("vc_lo", [P, TOK, HEAD_DIM], F32R)
        qT_hi, qT_lo = sb("qT_hi", [P, TOK, GROUP * P], F32R), sb("qT_lo", [P, TOK, GROUP * P], F32R)
        PT_hi, PT_lo = sb("PT_hi", [P, TOK, GROUP * P], F32R), sb("PT_lo", [P, TOK, GROUP * P], F32R)
        pT_hi = qT_hi[:, 0, :].rearrange("q (j t) -> q j t", j=PLE_T)
        pT_lo = qT_lo[:, 0, :].rearrange("q (j t) -> q j t", j=PLE_T)
        arena = sb("arena", [P, 10240])

        def at(a, size):
            return arena[:, a:a + size]

        kT = at(0, 2048).rearrange("q (h s) -> q h s", h=N_KV)
        v_sb = at(2048, 2048).rearrange("q (t n) -> q t n", t=TOK)
        bias = at(4096, 1536).rearrange("q (h s) -> q h s", h=GROUP)
        S = at(5632, 1024).rearrange("q (h s) -> q h s", h=GROUP)
        squares = at(5632, 1024)
        qk = at(6656, 1024).rearrange("q (t n) -> q t n", t=TOK)
        sg = qk
        oT = at(7680, 1024).rearrange("q (b n) -> q b n", b=TOK)
        xT_sq = [at(2048 * k, 2048).rearrange("q (j t) -> q j t", t=SEQ) for k in range(2)]
        sq_sum = at(5632, 1024).rearrange("q (j t) -> q j t", t=SEQ)
        dist_i = at(8832, 384).bitcast(I32)
        dist = at(9216, 384)
        x1 = at(0, 8192).rearrange("q (t n) -> q t n", t=TOK)
        xres = at(8192, 1024).rearrange("q (t n) -> q t n", t=TOK)
        p_in = at(9216, PLE_T * SEQ).rearrange("q (j t) -> q j t", j=PLE_T)
        junk = at(9216, 1024).rearrange("q (t n) -> q t n", t=TOK)

        ident = sb("ident", [P, P])
        g1T, g2T = sb("g1T", [P, KT]), sb("g2T", [P, KT])
        qgT, kgT = sb("qgT", [P, 1]), sb("kgT", [P, 1])
        ones = sb("ones", [P, 1])
        nsink = sb("nsink", [P, N_KV * GROUP])
        ss1 = sb("ss1", [P, TOK, NOUT])
        ssr = sb("ssr", [P, TOK])
        r = sb("r", [P, TOK])
        mhalf = sb("mhalf", [P, TOK * GROUP])
        one_half = sb("one_half", [P, GROUP])
        ssq = sb("ssq", [P, TOK * GROUP])
        rstd = sb("rstd", [P, TOK, GROUP])
        nm = sb("nm", [P, TOK, GROUP])
        sd = sb("sd", [P, TOK, GROUP])
        den = sb("den", [P, TOK, GROUP])
        rinv = sb("rinv", [P, TOK, GROUP])

        bank = [ctx.enter_context(nc.psum_tensor(f"bank{i}", [P, N], F32)) for i in range(8)]
        acc = [bank[0:2], bank[2:4]]

        raw_in = [sem(f"raw_in{i}") for i in range(RING)]
        hi_done, lo_done = sem("hi_done"), sem("lo_done")
        pe_half = sem("pe_half")
        acc_free = sem("acc_free")
        x_landed = [sem(f"x_landed{i}") for i in range(KT // 4)]
        g1_landed, vec_landed, sink_landed = sem("g1_landed"), sem("vec_landed"), sem("sink_landed")
        ident_zero, ident_ready = sem("ident_zero"), sem("ident_ready")
        iota_ready, dist_f, dist_neg = sem("iota_ready"), sem("dist_f"), sem("dist_neg")
        dist_mask, bias_ready = sem("dist_mask"), sem("bias_ready")
        consts_ready = sem("consts_ready")
        nsink_ready, table_loaded = sem("nsink_ready"), sem("table_loaded")
        xT_hi, xT_lo = sem("xT_hi"), sem("xT_lo")
        sq_ready, sq_added, sq_total = sem("sq_ready"), sem("sq_added"), sem("sq_total")
        ss_sum, mean_ready, r_ready = sem("ss_sum"), sem("mean_ready"), sem("r_ready")
        qk_sq, qk_ss, qk_mean, qk_rstd = sem("qk_sq"), sem("qk_ss"), sem("qk_mean"), sem("qk_rstd")
        k_normed, qk_tp, qk_T, qT_split = sem("k_normed"), sem("qk_tp"), sem("qk_T"), sem("qT_split")
        kv_hi, kv_lo = sem("kv_hi"), sem("kv_lo")
        scores_ps, scores_sb, rowmax, max_ready = (sem("scores_ps"), sem("scores_sb"), sem("rowmax"),
                                                   sem("max_ready"))
        sink_diff, exp_ready, probs_ready = sem("sink_diff"), sem("exp_ready"), sem("probs_ready")
        probs_tp, probs_hi, probs_lo = sem("probs_tp"), sem("probs_hi"), sem("probs_lo")
        den_sum, rinv_ready, o_ps, o_ready = sem("den_sum"), sem("rinv_ready"), sem("o_ps"), sem("o_ready")
        sg_ready, sz_tp, go_T = sem("sg_ready"), sem("sz_tp"), sem("go_T")
        conv_hi, conv_lo = sem("conv_hi"), sem("conv_lo")
        xres_in, x1_kept, x1_tp, x1_T, x1_sq = (sem("xres_in"), sem("x1_kept"), sem("x1_tp"), sem("x1_T"),
                                                sem("x1_sq"))
        p_landed, pT_top, pT_split = sem("p_landed"), sem("pT_top"), sem("pT_split")
        pool_sum = sem("pool_sum")
        proj_0 = sem("proj_0")
        gated_proj, out_ready = sem("gated_proj"), sem("out_ready")
        out_stored = sem("out_stored")

        block = ctx.enter_context(nc.Block())

        @block.sync
        def _(sp):
            def load(h, i, w, col):
                if not (isinstance(h, int) and h < RING):
                    sp.wait_ge(lo_done, h - (RING - 1))
                src = w[2 * P * i:2 * P * (i + 1), bass.ds(col, N)].rearrange("(a q) n -> q a n", q=P)
                dst = raw[:, i % RING, :].rearrange("q (a n) -> q a n", a=2)
                sp.dma_start(dst, src).then_inc(raw_in[i % RING], 16)

            def chunk(g, w, col):
                for i in range(HALVES):
                    load(g * HALVES + i, i, w, col)

            def load_x(k):
                src = xT[4 * P * k:4 * P * (k + 1), :].rearrange("(j q) t -> q j t", q=P)
                sp.dma_start(nextT[:, 4 * k:4 * k + 4, :], src).then_inc(x_landed[k], 16)

            x_after = {1: 1, 3: 2, 5: 4, 7: 5, 9: 6, 11: 7}
            load_x(0)
            for i in range(HALVES):
                load(i, i, w_in, Q_W)
                if i in x_after:
                    load_x(x_after[i])
                if i == 3:
                    load_x(3)
            with sp.Fori(1, G_Q0) as g:
                chunk(g, w_in, g * N + Q_W)
            chunk(G_Q0, w_in, 0)
            with sp.Fori(0, N_KV - 1) as c:
                chunk(c * 2 + G_Z(0), w_in, c * N + (Q_W + 2 * KV_W))
                chunk(c * 2 + (G_Z(0) + 1), w_in, c * N + N)
            chunk(G_Z(N_KV - 1), w_in, Q_W + 2 * KV_W + (N_KV - 1) * N)
            with sp.Fori(0, NOUT) as n:
                chunk(n + G_OUT, w_out, n * N)
            with sp.Fori(0, NOUT) as n:
                chunk(n + G_GATE, w_gate, n * N)
            for n in range(NOUT):
                sp.wait_ge(lo_done, G_PROJ * HALVES + n - (RING - 1))
                src = w_proj[:, n * N:(n + 1) * N].rearrange("(a q) n -> q a n", q=P)
                sp.dma_start(raw[:, n % RING, :].rearrange("q (a n) -> q a n", a=2), src)\
                  .then_inc(raw_in[n % RING], 16)
            for n in range(NOUT):
                cols = slice(n * N, (n + 1) * N)
                for t in range(TOK):
                    if n < POOL_SUMS:
                        sp.wait_ge(pool_sum, TOK * n + t + 1)
                    else:
                        sp.wait_ge(out_ready, TOK * (n - POOL_SUMS) + t + 1)
                    sp.dma_start(out[t * P:(t + 1) * P, cols], gates[:, t, cols]).then_inc(out_stored, 16)
            sp.wait_ge(out_stored, 16 * TOK * NOUT)

        @block.gpsimd
        def _(pool):
            pool.memset(ident[:, :], 0.0).then_inc(ident_zero, 1)
            pool.wait_ge(ident_zero, 1)
            pool.affine_select(out=ident[:, :], in_=ident[:, :], compare_op=ALU.not_equal, fill=1.0, base=0,
                               pattern=[[-1, P]], channel_multiplier=1).then_inc(ident_ready, 1)
            pool.memset(ones[:, :], 1.0).then_inc(consts_ready, 1)
            pool.memset(one_half[:, :], 0.5).then_inc(consts_ready, 1)
            pool.memset(mhalf[:, :], -0.5).then_inc(consts_ready, 1)
            pool.iota(dist_i, pattern=[[-1, 3 * P]], base=P, channel_multiplier=1).then_inc(iota_ready, 1)
            pool.wait_ge(dist_neg, 1)
            pool.affine_select(out=dist, in_=dist, compare_op=ALU.is_ge, fill=MASKED, base=P + WINDOW,
                               pattern=[[-1, 3 * P]], channel_multiplier=1).then_inc(dist_mask, 1)
            pool.wait_ge(dist_mask, 1)
            pool.affine_select(out=dist, in_=dist, compare_op=ALU.is_ge, fill=MASKED, base=WINDOW - P,
                               pattern=[[1, 3 * P]], channel_multiplier=-1).then_inc(dist_mask, 1)
            pool.wait_ge(dist_mask, 2)
            for h in range(GROUP):
                last = pool.tensor_scalar(bias[:, h, :], dist, 2.0 ** (-8.0 * (h + 1) / (N_KV * GROUP)), None,
                                          ALU.mult)
            last.then_inc(bias_ready, 1)
            pool.wait_ge(consts_ready, 3)

            rstd_flat = rstd[:, :, :].rearrange("q t h -> q (t h)")
            pool.wait_ge(mean_ready, 1)
            pool.tensor_tensor(r[:, :], ssr[:, :], mhalf[:, 0:TOK], ALU.pow).then_inc(r_ready, 1)
            for e in range(2):
                pool.wait_ge(qk_mean, e + 1)
                pool.tensor_tensor(rstd_flat, ssq[:, :], mhalf[:, :], ALU.pow).then_inc(qk_rstd, 1)

            def group(c):
                pool.wait_ge(qk_mean, c + 3)
                pool.tensor_tensor(rstd_flat, ssq[:, :], mhalf[:, :], ALU.pow).then_inc(qk_rstd, 1)

            with pool.Fori(0, N_KV - 1) as c:
                group(c)
                pool.wait_ge(scores_sb, c * 2 + 2)
                pool.tensor_tensor(bias, bias, one_half[:, :].unsqueeze(2).to_broadcast([P, GROUP, 3 * P]),
                                   ALU.mult).then_inc(bias_ready, 1)
            group(N_KV - 1)
            with pool.Fori(0, NOUT) as n:
                pool.wait_ge(acc_free, n + (G_OUT + 1))
                pool.tensor_copy(x1[:, :, bass.ds(n * N, N)], xres).then_inc(x1_kept, 1)
            pool.wait_ge(mean_ready, 2)
            pool.tensor_tensor(r[:, :], ssr[:, :], mhalf[:, 0:TOK], ALU.pow).then_inc(r_ready, 1)
            for n in range(POOL_SUMS):
                cols = slice(n * N, (n + 1) * N)
                for t in range(TOK):
                    pool.wait_ge(gated_proj, TOK * n + t + 1)
                    pool.tensor_tensor(gates[:, t, cols], gates[:, t, cols], x1[:, t, cols], ALU.add)\
                        .then_inc(pool_sum, 1)

        @block.scalar
        def _(act):
            def hi_half(g, i):
                act.wait_ge(raw_in[i % RING], g * (16 * HALVES // RING) + 16 * (i // RING + 1))
                if not (isinstance(g, int) and g == 0 and i < RING):
                    act.wait_ge(pe_half, g * HALVES + (i - RING + 1))
                nc.scalar.activation(w_hi[:, i % RING, :], raw[:, i % RING, :], ACT.Copy).then_inc(hi_done, 1)

            act.dma_start(g1T[:, :], norm_gT).then_inc(g1_landed, 16)
            act.wait_ge(consts_ready, 1)
            nc.scalar.activation(sd[:, 0, 0:1], ones[:, :], ACT.Copy).then_inc(table_loaded, 1)
            for dst, src in ((g2T, ple_gT), (qgT, q_gT), (kgT, k_gT)):
                act.dma_start(dst[:, :], src).then_inc(vec_landed, 16)
            act.dma_start(nsink[:, :], sink[0, :].partition_broadcast(P)).then_inc(sink_landed, 16)

            def xT_hi_pair(i):
                act.wait_ge(x_landed[i // 2], 16)
                for jj in range(2):
                    j = 2 * i + jj
                    last = nc.scalar.activation(aT_hi[:, j, :], nextT[:, j, :], ACT.Copy, scale=g1T[:, j:j + 1])
                last.then_inc(xT_hi, 1)

            def x_squares(m):
                act.wait_ge(x_landed[2 * m + 1], 16)
                if m >= 2:
                    act.wait_ge(sq_added, 2 * (m - 1) - 1)
                nc.scalar.activation(xT_sq[m % 2], nextT[:, 8 * m:8 * m + 8, :], ACT.Square).then_inc(sq_ready, 1)

            def k_transposed(e):
                act.wait_ge(qk_tp, e + 1)
                for t in range(TOK):
                    last = nc.scalar.activation(kT[:, 4 * e:4 * e + 4, t * P:(t + 1) * P],
                                                bank[4 + t][:, :].rearrange("q (h n) -> q h n", h=GROUP),
                                                ACT.Copy, scale=kgT[:, :])
                last.then_inc(qk_T, 1)

            def q_transposed(c):
                act.wait_ge(qk_tp, c + 3)
                for t in range(TOK):
                    last = nc.scalar.activation(qT_hi[:, t, :], bank[4 + t][:, :], ACT.Copy, scale=qgT[:, :])
                last.then_inc(qk_T, 1)

            def split_kv(c):
                nc.scalar.activation(kc_hi[:, :], kT[:, bass.ds(c, 1), :].rearrange("q a s -> q (a s)"), ACT.Copy)
                nc.scalar.activation(vc_hi[:, :, :], v_sb[:, :, bass.ds(c * HEAD_DIM, HEAD_DIM)], ACT.Copy)\
                  .then_inc(kv_hi, 1)

            def exps(c, b):
                act.wait_ge(max_ready, c * 2 + (b + 1))
                for h in range(GROUP):
                    nc.scalar.activation(S[:, h, :], S[:, h, :], ACT.Exp, bias=nm[:, b, h:h + 1],
                                         accum_out=den[:, b, h:h + 1])
                nc.scalar.activation(sd[:, b, :], sd[:, b, :], ACT.Exp).then_inc(exp_ready, 1)

            def probs_transposed(c, b):
                act.wait_ge(probs_tp, c * 2 + (b + 1))
                for s in range(TOK):
                    last = nc.scalar.activation(PT_hi[:, s, :], bank[4 + s][:, :], ACT.Copy)
                last.then_inc(probs_hi, 1)

            def outputs_transposed(c, b):
                act.wait_ge(o_ps, c * 2 + (b + 1))
                nc.scalar.activation(oT[:, b, :], bank[4][:, :], ACT.Copy).then_inc(o_ready, 1)

            def z_sigmoid(c):
                act.wait_ge(pe_half, (c * 2 + (G_Z(0) + 1)) * HALVES)
                for t in range(TOK):
                    last = nc.scalar.activation(sg[:, t, :], acc[1][t][:, :], ACT.Sigmoid, scale=r[:, t:t + 1])
                last.then_inc(sg_ready, 1)

            def convert_hi(i, g_before, written, count):
                act.wait_ge(pe_half, g_before * HALVES + i + 1)
                act.wait_ge(written, count)
                nc.scalar.activation(aT_hi[:, 2 * i:2 * i + 2, :], nextT[:, 2 * i:2 * i + 2, :], ACT.Copy)\
                  .then_inc(conv_hi, 1)

            def x1_transposed(n):
                act.wait_ge(x1_tp, n + 1)
                for jj in range(4):
                    b = bank[4 + jj // 2][:, (jj % 2) * SEQ:(jj % 2 + 1) * SEQ]
                    last = nc.scalar.activation(nextT[:, bass.ds(n * 4 + jj, 1), :].rearrange("q a t -> q (a t)"), b,
                                                ACT.Copy, scale=g2T[:, bass.ds(n * 4 + jj, 1)])
                last.then_inc(x1_T, 1)

            def x1_squares(n):
                act.wait_ge(acc_free, n + (G_OUT + 1))
                for t in range(TOK):
                    last = nc.scalar.activation(junk[:, t, :], xres[:, t, :], ACT.Square,
                                                accum_out=ss1[:, t, bass.ds(n, 1)])
                last.then_inc(x1_sq, 1)

            def load_residual(n):
                if not (isinstance(n, int) and n == 0):
                    act.wait_ge(x1_sq, n)
                    act.wait_ge(x1_kept, n)
                act.dma_start(xres, x[:, bass.ds(n * N, N)].rearrange("(t q) n -> q t n", q=P)).then_inc(xres_in, 16)

            def gate_sigmoid(n, pair):
                act.wait_ge(pe_half, (n + (G_GATE + 1)) * HALVES)
                for t in range(TOK):
                    last = nc.scalar.activation(gates[:, t, bass.ds(n * N, N)], acc[pair][t][:, :], ACT.Sigmoid,
                                                scale=r[:, t:t + 1])
                last.then_inc(acc_free, 1)

            act.wait_ge(g1_landed, 16)
            for i in range(HALVES):
                xT_hi_pair(i)
                hi_half(0, i)
                if i in (4, 7, 10, 13):
                    x_squares((i - 4) // 3)
            act.wait_ge(vec_landed, 48)
            for g in (1, 2, 3, 4):
                for i in range(HALVES):
                    hi_half(g, i)
                    if i == 8 and g <= 2:
                        k_transposed(g - 1)
                    elif i == 7 and g == 4:
                        act.wait_ge(qk_T, 2)
                        act.wait_ge(acc_free, 4)
                        split_kv(0)

            def attention(c, i):
                if i == 5:
                    q_transposed(c)
                elif i == 8:
                    exps(c, 0)
                elif i == 10:
                    probs_transposed(c, 0)
                elif i == 13:
                    exps(c, 1)
                    outputs_transposed(c, 0)
                elif i == 15:
                    probs_transposed(c, 1)

            def gating(c, i):
                if i == 1:
                    outputs_transposed(c, 1)
                elif i == 2:
                    z_sigmoid(c)

            with act.Fori(0, N_KV - 1) as c:
                for i in range(HALVES):
                    hi_half(c * 2 + G_Z(0), i)
                    attention(c, i)
                for i in range(HALVES):
                    hi_half(c * 2 + (G_Z(0) + 1), i)
                    gating(c, i)
                    if i == 9:
                        split_kv(c + 1)

            c = N_KV - 1
            for i in range(HALVES):
                hi_half(G_Z(c), i)
                attention(c, i)
                if i >= AHEAD:
                    convert_hi(i - AHEAD, G_Z(c), go_T, (i - AHEAD) // 2 + 1)
            for i in range(HALVES):
                hi_half(G_OUT, i)
                if i == 0:
                    act.dma_start(p_in, pT.rearrange("(j q) t -> q j t", q=P)).then_inc(p_landed, 16)
                gating(c, i)
                if i < 2:
                    convert_hi(12 + i, G_Z(c), go_T, (12 + i) // 2 + 1)
                elif i in (8, 9):
                    convert_hi(6 + i, G_Z(c), go_T, N_KV)
                elif i == 10:
                    act.wait_ge(go_T, N_KV)
                    load_residual(0)
                elif i == 11:
                    act.wait_ge(p_landed, 16)
                    nc.scalar.activation(pT_hi, p_in, ACT.Copy).then_inc(pT_top, 1)

            def out_chunk(n):
                for i in range(HALVES):
                    hi_half(n + G_OUT, i)
                    if i == 7:
                        x1_transposed(n - 1)
                    elif i == 9:
                        x1_squares(n - 1)
                    elif i == 10:
                        load_residual(n)

            act.wait_ge(conv_lo, HALVES)
            with act.Fori(1, NOUT - 1) as n:
                out_chunk(n)
            n = NOUT - 1
            for i in range(HALVES):
                hi_half(n + G_OUT, i)
                if i == 7:
                    x1_transposed(n - 1)
                elif i == 9:
                    x1_squares(n - 1)
                elif i == 10:
                    load_residual(n)
                if i >= AHEAD:
                    convert_hi(i - AHEAD, G_GATE - 1, x1_T, (i - AHEAD) // 2 + 1)
            for i in range(HALVES):
                hi_half(G_GATE, i)
                if i < 2:
                    convert_hi(12 + i, G_GATE - 1, x1_T, (12 + i) // 2 + 1)
                elif i == 7:
                    x1_transposed(NOUT - 1)
                elif i in (8, 9):
                    convert_hi(6 + i, G_GATE - 1, x1_T, NOUT)
                elif i == 10:
                    x1_squares(NOUT - 1)

            def gate_chunk(n, pair):
                for i in range(HALVES):
                    hi_half(n + G_GATE, i)
                    if i == 2:
                        gate_sigmoid(n - 1, pair)

            act.wait_ge(r_ready, 2)
            with act.Fori(0, NOUT // 2 - 1) as m:
                n = m * 2 + 1
                gate_chunk(n, 0)
                gate_chunk(n + 1, 1)
            gate_chunk(NOUT - 1, 0)

            for n in range(NOUT):
                hi_half(G_PROJ, n)
                if n == 2:
                    gate_sigmoid(NOUT - 1, 1)

        @block.vector
        def _(dve):
            def lo_half(g, i):
                dve.wait_ge(hi_done, g * HALVES + (i + 1))
                nc.vector.tensor_tensor(w_lo[:, i % RING, :], raw[:, i % RING, :],
                                        w_hi[:, i % RING, :].bitcast(F32), ALU.subtract).then_inc(lo_done, 1)

            dve.wait_ge(iota_ready, 1)
            nc.vector.tensor_copy(dist, dist_i).then_inc(dist_f, 1)
            dve.wait_ge(dist_f, 1)
            nc.vector.scalar_tensor_tensor(dist, dist, -1.0, dist, ALU.mult, ALU.min).then_inc(dist_neg, 1)
            dve.wait_ge(g1_landed, 16)

            def add_squares(k):
                m = (k + 1) // 2
                dve.wait_ge(sq_ready, m + 1)
                if k == 0:
                    a, b = xT_sq[0][:, 0:4, :], xT_sq[0][:, 4:8, :]
                else:
                    dve.wait_ge(sq_added, k)
                    a, b = sq_sum, xT_sq[m % 2][:, 4 * (1 - k % 2):4 * (1 - k % 2) + 4, :]
                nc.vector.tensor_tensor(sq_sum, a, b, ALU.add).then_inc(sq_added, 1)

            for i in range(HALVES):
                dve.wait_ge(xT_hi, i + 1)
                for jj in range(2):
                    j = 2 * i + jj
                    last = nc.vector.scalar_tensor_tensor(aT_lo[:, j, :], nextT[:, j, :], g1T[:, j:j + 1],
                                                          aT_hi[:, j, :].bitcast(F32), ALU.mult, ALU.subtract)
                last.then_inc(xT_lo, 1)
                lo_half(0, i)
                if i in SQUARE_STEPS:
                    add_squares(SQUARE_STEPS.index(i))

            def evacuate(g, pair, dsts):
                dve.wait_ge(pe_half, g * HALVES + HALVES)
                for t in range(TOK):
                    last = nc.vector.tensor_scalar(dsts[t], acc[pair][t][:, :], r[:, t:t + 1], None, ALU.mult)
                last.then_inc(acc_free, 1)

            def qk_squares(g):
                dve.wait_ge(acc_free, g + 1)
                flat = qk.rearrange("q t n -> q (t n)")
                nc.vector.tensor_tensor(squares, flat, flat, ALU.mult).then_inc(qk_sq, 1)

            def qk_sums(e, scale=1.0):
                dve.wait_ge(qk_sq, e + 1)
                nc.vector.tensor_reduce(ssq[:, :], squares.rearrange("q (h n) -> q h n", n=HEAD_DIM), X_AXIS,
                                        ALU.add).then_inc(qk_ss, 1)
                dve.wait_ge(qk_ss, e + 1)
                nc.vector.tensor_scalar(ssq[:, :], ssq[:, :], 1.0 / (HEAD_DIM * scale ** 2), EPS / scale ** 2, ALU.mult,
                                        ALU.add)\
                  .then_inc(qk_mean, 1)

            def split_kv(c):
                dve.wait_ge(kv_hi, c + 1)
                nc.vector.tensor_tensor(kc_lo[:, :], kT[:, bass.ds(c, 1), :].rearrange("q a s -> q (a s)"),
                                        kc_hi[:, :].bitcast(F32), ALU.subtract)
                nc.vector.tensor_tensor(vc_lo[:, :, :], v_sb[:, :, bass.ds(c * HEAD_DIM, HEAD_DIM)],
                                        vc_hi[:, :, :].bitcast(F32), ALU.subtract).then_inc(kv_lo, 1)

            dve.wait_ge(vec_landed, 48)
            dve.wait_ge(sink_landed, 16)
            nc.vector.tensor_scalar(nsink[:, :], nsink[:, :], -1.0, None, ALU.mult).then_inc(nsink_ready, 1)
            for g in (1, 2, 3, 4):
                for i in range(HALVES):
                    lo_half(g, i)
                    e = g - 1
                    if i == 1 and g == 1:
                        dve.wait_ge(sq_total, 1)
                        nc.vector.tensor_scalar(ssr[:, :], bank[6][:, 0:TOK], 1.0 / D_MODEL, EPS, ALU.mult, ALU.add)\
                          .then_inc(mean_ready, 1)
                    elif i == 3 and g == 1:
                        dve.wait_ge(r_ready, 1)
                    if i == 3 and g <= 2:
                        evacuate(e, e % 2, [qk[:, t, :] for t in range(TOK)])
                    elif i == 3:
                        evacuate(e, e % 2, [v_sb[:, t, (e - 2) * N:(e - 1) * N] for t in range(TOK)])
                    elif i == 4 and g <= 2:
                        qk_squares(e)
                        qk_sums(e)
                    elif i == 6 and g <= 2:
                        dve.wait_ge(qk_rstd, e + 1)
                        nc.vector.tensor_tensor(
                            qk.rearrange("q t (h n) -> q (t h) n", n=HEAD_DIM),
                            qk.rearrange("q t (h n) -> q (t h) n", n=HEAD_DIM),
                            rstd[:, :, :].rearrange("q t h -> q (t h)").unsqueeze(2)
                                .to_broadcast([P, TOK * GROUP, HEAD_DIM]), ALU.mult).then_inc(k_normed, 1)
                    elif i == 8 and g == 4:
                        split_kv(0)

            def q_lo(c):
                dve.wait_ge(qk_T, c + 3)
                for t in range(TOK):
                    last = nc.vector.scalar_tensor_tensor(qT_lo[:, t, :], bank[4 + t][:, :], qgT[:, :],
                                                          qT_hi[:, t, :].bitcast(F32), ALU.mult, ALU.subtract)
                last.then_inc(qT_split, 1)

            def score_rows(c, b):
                dve.wait_ge(scores_ps, c * 2 + (b + 1))
                if b == 0:
                    dve.wait_ge(bias_ready, c + 1)
                    dve.wait_ge(qk_rstd, c + 3)
                else:
                    dve.wait_ge(probs_tp, c * 2 + 1)
                for h in range(GROUP):
                    ps = bank[6 + h // 2][:, (h % 2) * SEQ:(h % 2 + 1) * SEQ]
                    last = nc.vector.scalar_tensor_tensor(S[:, h, :], ps, rstd[:, b, h:h + 1],
                                                          bias[:, h, P * (1 - b):P * (1 - b) + SEQ], ALU.mult, ALU.add)
                last.then_inc(scores_sb, 1)

            def maxima(c, b):
                k = c * 2 + (b + 1)
                dve.wait_ge(scores_sb, k)
                nc.vector.tensor_reduce(nm[:, b, :], S, X_AXIS, ALU.max, negate=True).then_inc(rowmax, 1)
                dve.wait_ge(rowmax, k)
                sinks = nsink[:, bass.ds(c * GROUP, GROUP)]
                nc.vector.tensor_tensor(nm[:, b, :], nm[:, b, :], sinks, ALU.min).then_inc(sink_diff, 1)
                dve.wait_ge(sink_diff, k)
                nc.vector.tensor_tensor(sd[:, b, :], nm[:, b, :], sinks, ALU.subtract).then_inc(max_ready, 1)

            def normalize(c, b):
                k = c * 2 + (b + 1)
                dve.wait_ge(exp_ready, k)
                nc.vector.tensor_tensor(den[:, b, :], den[:, b, :], sd[:, b, :], ALU.add).then_inc(den_sum, 1)
                dve.wait_ge(den_sum, k)
                nc.vector.reciprocal(rinv[:, b, :], den[:, b, :]).then_inc(rinv_ready, 1)
                dve.wait_ge(rinv_ready, k)
                nc.vector.tensor_tensor(S, S, rinv[:, b, :].unsqueeze(2).to_broadcast([P, GROUP, SEQ]), ALU.mult)\
                  .then_inc(probs_ready, 1)

            def probs_lo_part(c, b):
                dve.wait_ge(probs_hi, c * 2 + (b + 1))
                for s in range(TOK):
                    last = nc.vector.tensor_tensor(PT_lo[:, s, :], bank[4 + s][:, :], PT_hi[:, s, :].bitcast(F32),
                                                   ALU.subtract)
                last.then_inc(probs_lo, 1)

            def attention(c, i):
                g = c * 2 + G_Z(0)
                if i == 2:
                    evacuate(g - 1, 0, [qk[:, t, :] for t in range(TOK)])
                elif i == 3:
                    qk_squares(g - 1)
                elif i == 4:
                    qk_sums(c + 2, SCALE)
                elif i == 5:
                    q_lo(c)
                elif i == 6:
                    score_rows(c, 0)
                elif i == 7:
                    maxima(c, 0)
                elif i == 9:
                    normalize(c, 0)
                elif i == 10:
                    score_rows(c, 1)
                elif i == 11:
                    probs_lo_part(c, 0)
                elif i == 12:
                    maxima(c, 1)
                elif i == 14:
                    normalize(c, 1)

            def gating(c, i):
                if i == 0:
                    probs_lo_part(c, 1)
                elif i == 3:
                    dve.wait_ge(sg_ready, c + 1)
                    for t in range(TOK):
                        last = nc.vector.scalar_tensor_tensor(sg[:, t, :], acc[1][t][:, :], r[:, t:t + 1], sg[:, t, :],
                                                              ALU.mult, ALU.mult)
                    last.then_inc(acc_free, 1)
                elif i == 6:
                    dve.wait_ge(sz_tp, c + 1)
                    dve.wait_ge(o_ready, c * 2 + 2)
                    for jj in range(2):
                        heads = oT.rearrange("q b (h n) -> q h b n", h=GROUP)[:, 2 * jj:2 * jj + 2]
                        last = nc.vector.tensor_tensor(
                            nextT[:, bass.ds(c * 4 + 2 * jj, 2), :].rearrange("q h (b n) -> q h b n", b=TOK),
                            bank[4 + jj][:, :].rearrange("q (h b n) -> q h b n", h=2, b=TOK), heads, ALU.mult)
                    last.then_inc(go_T, 1)

            def convert_lo(k, i):
                dve.wait_ge(conv_hi, k)
                nc.vector.tensor_tensor(aT_lo[:, 2 * i:2 * i + 2, :], nextT[:, 2 * i:2 * i + 2, :],
                                        aT_hi[:, 2 * i:2 * i + 2, :].bitcast(F32), ALU.subtract).then_inc(conv_lo, 1)

            with dve.Fori(0, N_KV - 1) as c:
                for i in range(HALVES):
                    lo_half(c * 2 + G_Z(0), i)
                    attention(c, i)
                for i in range(HALVES):
                    lo_half(c * 2 + (G_Z(0) + 1), i)
                    gating(c, i)
                    if i == 10:
                        split_kv(c + 1)
            c = N_KV - 1
            for i in range(HALVES):
                lo_half(G_Z(c), i)
                attention(c, i)
                if i >= AHEAD:
                    convert_lo(i - AHEAD + 1, i - AHEAD)
            for i in range(HALVES):
                lo_half(G_OUT, i)
                gating(c, i)
                if i < 2:
                    convert_lo(13 + i, 12 + i)
                elif i in (8, 9):
                    convert_lo(7 + i, 6 + i)
                elif i == 12:
                    dve.wait_ge(pT_top, 1)
                    nc.vector.tensor_tensor(pT_lo, p_in, pT_hi.bitcast(F32), ALU.subtract)\
                      .then_inc(pT_split, 1)

            def residual(n, pair):
                dve.wait_ge(pe_half, (n + (G_OUT + 1)) * HALVES)
                dve.wait_ge(xres_in, n * 16 + 16)
                for t in range(TOK):
                    last = nc.vector.tensor_tensor(xres[:, t, :], acc[pair][t][:, :], xres[:, t, :], ALU.add)
                last.then_inc(acc_free, 1)

            with dve.Fori(0, NOUT // 2 - 1) as m:
                n = m * 2 + 1
                for k in range(2):
                    for i in range(HALVES):
                        lo_half(n + (G_OUT + k), i)
                        if i == 2:
                            residual(n + (k - 1), k)
            for i in range(HALVES):
                lo_half(G_OUT + NOUT - 1, i)
                if i == 2:
                    residual(NOUT - 2, 0)
                if i >= AHEAD:
                    convert_lo(HALVES + i - AHEAD + 1, i - AHEAD)
            for i in range(HALVES):
                lo_half(G_GATE, i)
                if i < 2:
                    convert_lo(HALVES + 13 + i, 12 + i)
                if i == 2:
                    residual(NOUT - 1, 1)
                elif i == 12:
                    dve.wait_ge(x1_sq, NOUT)
                    nc.vector.tensor_reduce(ssr[:, :], ss1[:, :, :], X_AXIS, ALU.add).then_inc(ss_sum, 1)
                    dve.wait_ge(ss_sum, 1)
                    nc.vector.tensor_scalar(ssr[:, :], ssr[:, :], 1.0 / D_MODEL, EPS, ALU.mult, ALU.add)\
                      .then_inc(mean_ready, 1)
                if i in (8, 9):
                    convert_lo(HALVES + 7 + i, 6 + i)

            with dve.Fori(1, NOUT) as n:
                for i in range(HALVES):
                    lo_half(n + G_GATE, i)

            def gate_projection(n):
                dve.wait_ge(pe_half, G_PROJ * HALVES + n + 1)
                for t in range(TOK):
                    part = gates[:, t, n * N:(n + 1) * N]
                    nc.vector.tensor_tensor(part, acc[n % 2][t][:, :], part, ALU.mult).then_inc(gated_proj, 1)

            def last_output(n):
                for t in range(TOK):
                    if t == 0:
                        dve.wait_ge(proj_0, 1)
                    else:
                        dve.wait_ge(pe_half, G_PROJ * HALVES + n + 1)
                    part = gates[:, t, n * N:(n + 1) * N]
                    nc.vector.tensor_tensor(part, acc[n % 2][t][:, :], part, ALU.mult).then_inc(gated_proj, 1)
                    dve.wait_ge(gated_proj, TOK * n + t + 1)
                    nc.vector.tensor_tensor(part, part, x1[:, t, n * N:(n + 1) * N], ALU.add).then_inc(out_ready, 1)

            dve.wait_ge(acc_free, G_PROJ - 1)
            for n in range(NOUT):
                lo_half(G_PROJ, n)
                if n >= AHEAD - 1:
                    gate_projection(n - (AHEAD - 1))
            for n in range(NOUT - (AHEAD - 1), NOUT - 1):
                gate_projection(n)
            dve.wait_ge(x1_kept, NOUT)
            dve.wait_ge(acc_free, G_PROJ)
            last_output(NOUT - 1)

        @block.tensor
        def _(pe):
            def products(outs, hi_of, lo_of, i, first, final):
                for jj in range(2):
                    whi = w_hi[:, i % RING, jj * N:(jj + 1) * N]
                    wlo = w_lo[:, i % RING, jj * N:(jj + 1) * N]
                    for t in range(TOK):
                        ahi, alo = hi_of(jj, t), lo_of(jj, t)
                        nc.tensor.matmul(outs[t][:, :], ahi, wlo, start=first and jj == 0, stop=False)
                        nc.tensor.matmul(outs[t][:, :], ahi, whi, start=False, stop=False)
                        last = nc.tensor.matmul(outs[t][:, :], alo, whi, start=False, stop=final and jj == 1)
                last.then_inc(pe_half, 1)

            def half(g, i, pair):
                pe.wait_ge(lo_done, g * HALVES + (i + 1))
                products(acc[pair], lambda jj, t: aT_hi[:, 2 * i + jj, t * P:(t + 1) * P],
                         lambda jj, t: aT_lo[:, 2 * i + jj, t * P:(t + 1) * P], i, i == 0, i == HALVES - 1)

            def transpose_tokens(src, banks, done):
                for t in range(TOK):
                    for h in range(GROUP):
                        last = nc.tensor.transpose(banks[t][:, h * P:(h + 1) * P], src[:, t, h * P:(h + 1) * P],
                                                   ident[:, :])
                last.then_inc(done, 1)

            def transpose_columns(src, banks, done):
                for j in range(4):
                    for t in range(TOK):
                        last = nc.tensor.transpose(banks[j // 2][:, (j % 2) * SEQ + t * P:(j % 2) * SEQ + (t + 1) * P],
                                                   src[:, t, j * P:(j + 1) * P], ident[:, :])
                last.then_inc(done, 1)

            for i in range(HALVES):
                pe.wait_ge(xT_lo, i + 1)
                half(0, i, 0)
            pe.wait_ge(consts_ready, 1)
            pe.wait_ge(sq_added, 7)
            for t in range(TOK):
                for j in range(4):
                    last = nc.tensor.matmul(bank[6][:, t:t + 1], sq_sum[:, j, t * P:(t + 1) * P], ones[:, :],
                                            start=(j == 0), stop=(j == 3))
            last.then_inc(sq_total, 1)

            for g in (1, 2, 3, 4):
                if g >= 2:
                    pe.wait_ge(acc_free, g - 1)
                for i in range(HALVES):
                    half(g, i, g % 2)
                    if i == 5 and g <= 2:
                        pe.wait_ge(k_normed, g)
                        if g == 2:
                            pe.wait_ge(qk_T, 1)
                        transpose_tokens(qk, bank[4:6], qk_tp)

            def scores(c, b):
                if b == 0:
                    pe.wait_ge(kv_lo, c + 1)
                    pe.wait_ge(qT_split, c + 1)
                else:
                    pe.wait_ge(scores_sb, c * 2 + 1)
                for h in range(GROUP):
                    ps = bank[6 + h // 2][:, (h % 2) * SEQ:(h % 2 + 1) * SEQ]
                    qhi, qlo = qT_hi[:, b, h * P:(h + 1) * P], qT_lo[:, b, h * P:(h + 1) * P]
                    nc.tensor.matmul(ps, qhi, kc_lo[:, :], start=True, stop=False)
                    nc.tensor.matmul(ps, qhi, kc_hi[:, :], start=False, stop=False)
                    last = nc.tensor.matmul(ps, qlo, kc_hi[:, :], start=False, stop=True)
                last.then_inc(scores_ps, 1)

            def transpose_probs(c, b):
                pe.wait_ge(probs_ready, c * 2 + (b + 1))
                if b == 1:
                    pe.wait_ge(o_ready, c * 2 + 1)
                for s in range(TOK):
                    for h in range(GROUP):
                        last = nc.tensor.transpose(bank[4 + s][:, h * P:(h + 1) * P], S[:, h, s * P:(s + 1) * P],
                                                   ident[:, :])
                last.then_inc(probs_tp, 1)

            def head_values(c, b):
                pe.wait_ge(probs_lo, c * 2 + (b + 1))
                for s in range(TOK):
                    nc.tensor.matmul(bank[4][:, :], vc_hi[:, s, :], PT_lo[:, s, :], start=(s == 0), stop=False)
                    nc.tensor.matmul(bank[4][:, :], vc_hi[:, s, :], PT_hi[:, s, :], start=False, stop=False)
                    last = nc.tensor.matmul(bank[4][:, :], vc_lo[:, s, :], PT_hi[:, s, :], start=False,
                                            stop=(s == TOK - 1))
                last.then_inc(o_ps, 1)

            def attention(c, i):
                if i == 1:
                    pe.wait_ge(acc_free, c * 2 + G_Z(0))
                    transpose_tokens(qk, bank[4:6], qk_tp)
                elif i == 3:
                    scores(c, 0)
                elif i == 5:
                    scores(c, 1)
                elif i == 7:
                    transpose_probs(c, 0)
                elif i == 10:
                    head_values(c, 0)
                elif i == 12:
                    transpose_probs(c, 1)
                elif i == 14:
                    head_values(c, 1)

            def gating(c, i):
                if i == 3:
                    pe.wait_ge(acc_free, c * 2 + (G_Z(0) + 1))
                    pe.wait_ge(o_ready, c * 2 + 2)
                    transpose_columns(sg, bank[4:6], sz_tp)

            with pe.Fori(0, N_KV - 1) as c:
                g = c * 2 + G_Z(0)
                pe.wait_ge(acc_free, g - 1)
                for i in range(HALVES):
                    half(g, i, 1)
                    attention(c, i)
                pe.wait_ge(acc_free, g)
                for i in range(HALVES):
                    half(g + 1, i, 0)
                    gating(c, i)
            c = N_KV - 1
            pe.wait_ge(acc_free, G_Z(c) - 1)
            for i in range(HALVES):
                half(G_Z(c), i, 1)
                attention(c, i)
            pe.wait_ge(acc_free, G_OUT - 1)
            for i in range(HALVES):
                pe.wait_ge(conv_lo, i + 1)
                half(G_OUT, i, 0)
                gating(c, i)

            def x1_transpose(n):
                pe.wait_ge(acc_free, n + (G_OUT + 1))
                transpose_columns(xres, bank[4:6], x1_tp)

            with pe.Fori(0, NOUT // 2 - 1) as m:
                n = m * 2 + 1
                for k in range(2):
                    pe.wait_ge(acc_free, n + (G_OUT + k - 1))
                    for i in range(HALVES):
                        half(n + (G_OUT + k), i, (1 + k) % 2)
                        if i == 4:
                            x1_transpose(n + (k - 1))
            pe.wait_ge(acc_free, G_GATE - 2)
            for i in range(HALVES):
                half(G_GATE - 1, i, 1)
                if i == 4:
                    x1_transpose(NOUT - 2)

            pe.wait_ge(acc_free, G_GATE - 1)
            for i in range(HALVES):
                pe.wait_ge(conv_lo, HALVES + i + 1)
                half(G_GATE, i, 0)
                if i == 4:
                    x1_transpose(NOUT - 1)
            with pe.Fori(0, NOUT // 2 - 1) as m:
                n = m * 2 + 1
                for k in range(2):
                    pe.wait_ge(acc_free, n + (G_GATE + k - 1))
                    for i in range(HALVES):
                        half(n + (G_GATE + k), i, (1 + k) % 2)
            pe.wait_ge(acc_free, G_PROJ - 2)
            for i in range(HALVES):
                half(G_PROJ - 1, i, 1)

            pe.wait_ge(pT_split, 1)
            for n in range(NOUT):
                pe.wait_ge(lo_done, G_PROJ * HALVES + n + 1)
                if n < 2:
                    pe.wait_ge(acc_free, G_PROJ - 1 + n)
                else:
                    pe.wait_ge(gated_proj, TOK * (n - 1))
                if n == NOUT - 1:
                    for t in range(TOK):
                        for jj in range(PLE_T):
                            whi = w_hi[:, n % RING, jj * N:(jj + 1) * N]
                            wlo = w_lo[:, n % RING, jj * N:(jj + 1) * N]
                            phi, plo = pT_hi[:, jj, t * P:(t + 1) * P], pT_lo[:, jj, t * P:(t + 1) * P]
                            nc.tensor.matmul(acc[n % 2][t][:, :], phi, wlo, start=(jj == 0), stop=False)
                            nc.tensor.matmul(acc[n % 2][t][:, :], phi, whi, start=False, stop=False)
                            last = nc.tensor.matmul(acc[n % 2][t][:, :], plo, whi, start=False, stop=(jj == PLE_T - 1))
                        last.then_inc(pe_half if t else proj_0, 1)
                    break
                products(acc[n % 2], lambda jj, t: pT_hi[:, jj, t * P:(t + 1) * P],
                         lambda jj, t: pT_lo[:, jj, t * P:(t + 1) * P], n, True, True)


def kernel(**inputs):
    import numpy as _np
    import concourse.bacc as _bacc
    from concourse import mybir as _mybir
    from concourse.bass_utils import run_bass_kernel_spmd as _run

    given = {name: _np.asarray(inputs[name]) for name in (
        "x", "p", "norm_g", "attn_w_in", "attn_q_norm_g", "attn_k_norm_g", "attn_sink", "attn_w_out", "ple_norm_g",
        "ple_w_gate", "ple_w_proj")}
    laid_out = {
        "x": given["x"],
        "xT": given["x"][0].T,
        "pT": given["p"][0, 0].T,
        "norm_gT": given["norm_g"][0].reshape(KT, P).T,
        "w_in": given["attn_w_in"],
        "q_gT": given["attn_q_norm_g"].T,
        "k_gT": given["attn_k_norm_g"].T,
        "sink": given["attn_sink"],
        "w_out": given["attn_w_out"],
        "ple_gT": given["ple_norm_g"][0].reshape(KT, P).T,
        "w_gate": given["ple_w_gate"],
        "w_proj": given["ple_w_proj"],
    }
    nc = _bacc.Bacc("TRN2", target_bir_lowering=False, num_devices=1)
    arrays, args = {}, {}
    for name, a in laid_out.items():
        a = _np.ascontiguousarray(a)
        arrays[f"in_{name}_dram"] = a
        args[name] = nc.dram_tensor(f"in_{name}_dram", a.shape, _mybir.dt.from_np(a.dtype), kind="ExternalInput").ap()
    result = nc.dram_tensor("out_dram", (1, SEQ, D_MODEL), _mybir.dt.float32, kind="ExternalOutput").ap()
    encoder_layer(nc, **args, out=result)
    r = _run(nc, [arrays], core_ids=[0])
    return r.results[0]["out_dram"]
```
